# Optimizing a Trainium2 kernel written in Bass

```python
import math
import jax, jax.numpy as jnp
from jax import lax
import numpy as np

D_MODEL = 1024
BATCH = 1
SEQ = 256
DEPTH = 2

GRID_W = 64
CTX_LEN = 256
D_SSM = 512
SSM_GROUP = 16
N_SSM_GROUPS = D_SSM // SSM_GROUP
SSM_STATE = 64
D_CONV = 512
CONV_WIDTH = 31
CONV_PAD = CONV_WIDTH // 2
D_MIX = D_SSM + D_CONV
D_IN = D_SSM + 2 * D_CONV
D_FF = 2816
N_EXPERTS = 8
TOP_K = 2
D_FF_EXPERT = 2816
N_MOD = 6
EPS = 1e-6
DT_MIN = 1e-3
DT_MAX = 1e-1

kernel_name = "hybrid_s5_conformer_moe_dit"

def rmsnorm(x, g):
    x32 = x.astype(jnp.float32)
    y = x32 * lax.rsqrt(jnp.mean(x32 * x32, axis=-1, keepdims=True) + EPS)
    return (y * g.astype(jnp.float32)).astype(x.dtype)

def layernorm(x, g, b):
    x32 = x.astype(jnp.float32)
    mu = jnp.mean(x32, axis=-1, keepdims=True)
    xc = x32 - mu
    y = xc * lax.rsqrt(jnp.mean(xc * xc, axis=-1, keepdims=True) + EPS)
    return (y * g.astype(jnp.float32) + b.astype(jnp.float32)).astype(x.dtype)

def modulate(h, shift, scale):
    return h * (1 + scale) + shift

def s5_discretize(lam_re, lam_im, log_dt, b_re, b_im):
    lam = lax.complex(lam_re.astype(jnp.float32), lam_im.astype(jnp.float32))
    dt = jnp.exp(log_dt.astype(jnp.float32))[:, None]
    lam_bar = jnp.exp(lam * dt)
    b = lax.complex(b_re.astype(jnp.float32), b_im.astype(jnp.float32))
    b_bar = ((lam_bar - 1.0) / lam)[..., None] * b
    return lam_bar, b_bar

def diag_scan(lam_bar, bu, h0, reverse):
    if h0 is not None:
        idx = bu.shape[1] - 1 if reverse else 0
        bu = bu.at[:, idx].add(lam_bar * h0)
    a = jnp.broadcast_to(lam_bar, bu.shape)

    def combine(left, right):
        a_l, b_l = left
        a_r, b_r = right
        return a_l * a_r, a_r * b_l + b_r

    _, h = lax.associative_scan(combine, (a, bu), reverse=reverse, axis=1)
    return h

def s5_glu(y, d_skip, u, w_glu, b_glu, dtype):
    y = y + d_skip.astype(jnp.float32) * u.astype(jnp.float32)
    z = jax.nn.gelu(y)
    out = z * jax.nn.sigmoid(z @ w_glu.astype(jnp.float32) + b_glu.astype(jnp.float32))
    return out.astype(dtype)

def s5_bidirectional(u_lat, u_ctx, lam_re, lam_im, log_dt, b_re, b_im, c_re, c_im,
                     d_skip, w_glu, b_glu, need_ctx):
    dtype = u_lat.dtype

    def to_groups(u):
        return u.astype(jnp.float32).reshape(u.shape[0], u.shape[1], N_SSM_GROUPS, SSM_GROUP).astype(jnp.complex64)

    ug_lat, ug_ctx = to_groups(u_lat), to_groups(u_ctx)
    y_lat = jnp.zeros(u_lat.shape, jnp.float32)
    y_ctx = jnp.zeros(u_ctx.shape, jnp.float32)
    for direction in range(2):
        reverse = direction == 1
        lam_bar, b_bar = s5_discretize(lam_re[direction], lam_im[direction], log_dt[direction],
                                       b_re[direction], b_im[direction])
        cmat = lax.complex(c_re[direction].astype(jnp.float32), c_im[direction].astype(jnp.float32))
        s_ctx = diag_scan(lam_bar, jnp.einsum('blgh,gph->blgp', ug_ctx, b_bar), None, reverse)
        s_end = s_ctx[:, 0] if reverse else s_ctx[:, -1]
        s_lat = diag_scan(lam_bar, jnp.einsum('blgh,gph->blgp', ug_lat, b_bar), s_end, reverse)
        y_lat = y_lat + jnp.einsum('blgp,ghp->blgh', s_lat, cmat).real.reshape(u_lat.shape)
        if need_ctx:
            y_ctx = y_ctx + jnp.einsum('blgp,ghp->blgh', s_ctx, cmat).real.reshape(u_ctx.shape)
    out_lat = s5_glu(y_lat, d_skip, u_lat, w_glu, b_glu, dtype)
    out_ctx = s5_glu(y_ctx, d_skip, u_ctx, w_glu, b_glu, dtype) if need_ctx else None
    return out_lat, out_ctx

def conformer_conv(v, g, w_dw, b_dw, ln_g, ln_b):
    a = v * jax.nn.sigmoid(g)
    y = lax.conv_general_dilated(a, w_dw[:, None, :].astype(a.dtype), window_strides=(1,),
                                 padding=[(CONV_PAD, CONV_PAD)],
                                 dimension_numbers=('NWC', 'WIO', 'NWC'),
                                 feature_group_count=D_CONV) + b_dw
    return jax.nn.silu(layernorm(y, ln_g, ln_b))

def hybrid_mixer(a_lat, a_ctx, w_in, lam_re, lam_im, log_dt, b_re, b_im, c_re, c_im, d_skip,
                 w_glu, b_glu, conv_w, conv_b, ln_g, ln_b, w_out, need_ctx):
    p_lat = a_lat @ w_in
    p_ctx = a_ctx @ w_in
    s_lat, s_ctx = s5_bidirectional(p_lat[..., :D_SSM], p_ctx[..., :D_SSM], lam_re, lam_im, log_dt,
                                    b_re, b_im, c_re, c_im, d_skip, w_glu, b_glu, need_ctx)
    cv_lat = conformer_conv(p_lat[..., D_SSM:D_SSM + D_CONV], p_lat[..., D_SSM + D_CONV:],
                            conv_w, conv_b, ln_g, ln_b)
    y_lat = jnp.concatenate([s_lat, cv_lat], axis=-1) @ w_out
    if not need_ctx:
        return y_lat, None
    cv_ctx = conformer_conv(p_ctx[..., D_SSM:D_SSM + D_CONV], p_ctx[..., D_SSM + D_CONV:],
                            conv_w, conv_b, ln_g, ln_b)
    y_ctx = jnp.concatenate([s_ctx, cv_ctx], axis=-1) @ w_out
    return y_lat, y_ctx

def swiglu(h, w_gate, w_up, w_down):
    return (jax.nn.silu(h @ w_gate) * (h @ w_up)) @ w_down

def moe_swiglu(h, w_router, b_router, w_gate, w_up, w_down):
    logits = (h @ w_router).astype(jnp.float32) + b_router.astype(jnp.float32)
    top_v, top_i = lax.top_k(logits, TOP_K)
    top_w = jax.nn.softmax(top_v, axis=-1)
    gates = jnp.sum(jax.nn.one_hot(top_i, N_EXPERTS, dtype=jnp.float32) * top_w[..., None], axis=-2)
    gates = gates.astype(h.dtype)
    out = jnp.zeros(h.shape, h.dtype)
    for e in range(N_EXPERTS):
        out = out + gates[..., e:e + 1] * swiglu(h, w_gate[e], w_up[e], w_down[e])
    return out

def setup_inputs(seed: int = 0) -> dict:
    key = jax.random.key(seed)
    ks = iter(jax.random.split(key, 48))
    f32 = jnp.float32

    def nrm(shape, s):
        return s * jax.random.normal(next(ks), shape, f32)

    n_dense = (DEPTH + 1) // 2
    n_moe = DEPTH // 2
    G, P, H = N_SSM_GROUPS, SSM_STATE, SSM_GROUP
    return {
        "x": nrm((BATCH, SEQ, D_MODEL), 1.0),
        "c": nrm((BATCH, D_MODEL), 1.0),
        "ctx": nrm((BATCH, CTX_LEN, D_MODEL), 1.0),
        "c_ctx": nrm((D_MODEL,), 1.0),
        "w_ada": nrm((DEPTH, D_MODEL, N_MOD * D_MODEL), 0.5 * D_MODEL ** -0.5),
        "b_ada": nrm((DEPTH, N_MOD * D_MODEL), 0.02),
        "g_pre_mix": 1.0 + nrm((DEPTH, D_MODEL), 0.05),
        "g_post_mix": 1.0 + nrm((DEPTH, D_MODEL), 0.05),
        "g_pre_ffn": 1.0 + nrm((DEPTH, D_MODEL), 0.05),
        "g_post_ffn": 1.0 + nrm((DEPTH, D_MODEL), 0.05),
        "w_in": nrm((DEPTH, D_MODEL, D_IN), D_MODEL ** -0.5),
        "ssm_lam_re": -0.5 + nrm((DEPTH, 2, G, P), 0.01),
        "ssm_lam_im": jnp.pi * jnp.arange(P, dtype=f32) + nrm((DEPTH, 2, G, P), 0.01),
        "ssm_log_dt": jax.random.uniform(next(ks), (DEPTH, 2, G), f32, math.log(DT_MIN), math.log(DT_MAX)),
        "ssm_b_re": nrm((DEPTH, 2, G, P, H), (2 * H) ** -0.5),
        "ssm_b_im": nrm((DEPTH, 2, G, P, H), (2 * H) ** -0.5),
        "ssm_c_re": nrm((DEPTH, 2, G, H, P), (2 * P) ** -0.5),
        "ssm_c_im": nrm((DEPTH, 2, G, H, P), (2 * P) ** -0.5),
        "ssm_d": nrm((DEPTH, D_SSM), 1.0),
        "ssm_w_glu": nrm((DEPTH, D_SSM, D_SSM), D_SSM ** -0.5),
        "ssm_b_glu": nrm((DEPTH, D_SSM), 0.02),
        "conv_w": nrm((DEPTH, CONV_WIDTH, D_CONV), CONV_WIDTH ** -0.5),
        "conv_b": nrm((DEPTH, D_CONV), 0.02),
        "conv_ln_g": 1.0 + nrm((DEPTH, D_CONV), 0.05),
        "conv_ln_b": nrm((DEPTH, D_CONV), 0.02),
        "w_out": nrm((DEPTH, D_MIX, D_MODEL), D_MIX ** -0.5),
        "ffn_w_gate": nrm((n_dense, D_MODEL, D_FF), D_MODEL ** -0.5),
        "ffn_w_up": nrm((n_dense, D_MODEL, D_FF), D_MODEL ** -0.5),
        "ffn_w_down": nrm((n_dense, D_FF, D_MODEL), D_FF ** -0.5),
        "moe_w_router": nrm((n_moe, D_MODEL, N_EXPERTS), D_MODEL ** -0.5),
        "moe_b_router": nrm((n_moe, N_EXPERTS), 0.01),
        "moe_w_gate": nrm((n_moe, N_EXPERTS, D_MODEL, D_FF_EXPERT), D_MODEL ** -0.5),
        "moe_w_up": nrm((n_moe, N_EXPERTS, D_MODEL, D_FF_EXPERT), D_MODEL ** -0.5),
        "moe_w_down": nrm((n_moe, N_EXPERTS, D_FF_EXPERT, D_MODEL), D_FF_EXPERT ** -0.5),
    }

def reference(x, c, ctx, c_ctx, w_ada, b_ada, g_pre_mix, g_post_mix, g_pre_ffn, g_post_ffn, w_in,
              ssm_lam_re, ssm_lam_im, ssm_log_dt, ssm_b_re, ssm_b_im, ssm_c_re, ssm_c_im, ssm_d,
              ssm_w_glu, ssm_b_glu, conv_w, conv_b, conv_ln_g, conv_ln_b, w_out,
              ffn_w_gate, ffn_w_up, ffn_w_down, moe_w_router, moe_b_router, moe_w_gate, moe_w_up, moe_w_down):
    silu_c = jax.nn.silu(c)[:, None, :]
    silu_cc = jax.nn.silu(c_ctx)[None, None, :]
    h_lat, h_ctx = x, ctx
    for l in range(DEPTH):
        need_ctx = l < DEPTH - 1
        mod_lat = jnp.split(silu_c @ w_ada[l] + b_ada[l], N_MOD, axis=-1)
        mod_ctx = jnp.split(silu_cc @ w_ada[l] + b_ada[l], N_MOD, axis=-1)

        a_lat = modulate(rmsnorm(h_lat, g_pre_mix[l]), mod_lat[0], mod_lat[1])
        a_ctx = modulate(rmsnorm(h_ctx, g_pre_mix[l]), mod_ctx[0], mod_ctx[1])
        y_lat, y_ctx = hybrid_mixer(a_lat, a_ctx, w_in[l], ssm_lam_re[l], ssm_lam_im[l], ssm_log_dt[l],
                                    ssm_b_re[l], ssm_b_im[l], ssm_c_re[l], ssm_c_im[l], ssm_d[l],
                                    ssm_w_glu[l], ssm_b_glu[l], conv_w[l], conv_b[l], conv_ln_g[l],
                                    conv_ln_b[l], w_out[l], need_ctx)
        h_lat = h_lat + mod_lat[2] * rmsnorm(y_lat, g_post_mix[l])
        if need_ctx:
            h_ctx = h_ctx + mod_ctx[2] * rmsnorm(y_ctx, g_post_mix[l])

        f_lat = modulate(rmsnorm(h_lat, g_pre_ffn[l]), mod_lat[3], mod_lat[4])
        if l % 2 == 0:
            i = l // 2
            ffn = lambda h, i=i: swiglu(h, ffn_w_gate[i], ffn_w_up[i], ffn_w_down[i])
        else:
            i = l // 2
            ffn = lambda h, i=i: moe_swiglu(h, moe_w_router[i], moe_b_router[i], moe_w_gate[i],
                                            moe_w_up[i], moe_w_down[i])
        h_lat = h_lat + mod_lat[5] * rmsnorm(ffn(f_lat), g_post_ffn[l])
        if need_ctx:
            f_ctx = modulate(rmsnorm(h_ctx, g_pre_ffn[l]), mod_ctx[3], mod_ctx[4])
            h_ctx = h_ctx + mod_ctx[5] * rmsnorm(ffn(f_ctx), g_post_ffn[l])
    return h_lat


_drawn_inputs = setup_inputs


def setup_inputs(seed=0):
    import zlib

    import numpy as np

    out = dict(_drawn_inputs(seed))
    spreads = {}
    factors = {'ctx': 34.79,
     'c_ctx': 31.432,
     'ssm_lam_re': 39.102,
     'ssm_b_glu': 8.0,
     'conv_ln_b': 3.591,
     'moe_b_router': 4.301,
     'ssm_b_re': 3.178,
     'ssm_b_im': 3.179,
     'ssm_c_im': 3.546}
    for name, (base, spread) in spreads.items():
        noise = np.random.default_rng([zlib.crc32(name.encode()), seed]).standard_normal(out[name].shape)
        drawn = base * np.exp(spread * noise) if base else spread * noise
        out[name] = __import__('jax').numpy.asarray(drawn.astype(out[name].dtype))
    for name, factor in factors.items():
        out[name] = (out[name] * factor).astype(out[name].dtype)
    return out
```

```python
from contextlib import ExitStack

import concourse.bass as bass
from concourse import mybir

ALU = mybir.AluOpType
ACT = mybir.ActivationFunctionType
AX_X = mybir.AxisListType.X
F32 = mybir.dt.float32
I32 = mybir.dt.int32
U32 = mybir.dt.uint32

P = 128
HP = 64
TWO_PI = 6.283185307179586
PI = 3.1415925
ROUND = 12582912.0
TWO_PI_HI = 6.28125
TWO_PI_MID = 0.0019350051879882812
TWO_PI_LO = 3.0199159819e-07
UNROUTED = 1024.0


def hybrid_backbone(nc, x, c, ctx_in, c_ctx, w_ada, b_ada, g_pre_mix, g_post_mix, g_pre_ffn, g_post_ffn, w_in,
                    lam_re, lam_im, log_dt, b_re, b_im, c_re, c_im, ssm_d, w_glu, b_glu, conv_w, conv_b,
                    ln_g, ln_b, w_out, ffn_gate, ffn_up, ffn_down, router_w, router_b, moe_gate, moe_up,
                    moe_down, out):
    _, S, D = x.shape
    T = 2 * S
    L = w_ada.shape[0]
    KC = D // P
    DS = ssm_d.shape[1]
    MC = DS // P
    G, NS, GH = b_re.shape[2:]
    Q = G // 2
    HQ = Q // 2
    CL = P // GH
    NJ = T // CL
    NB = 8
    CW = conv_w.shape[1]
    PAD = CW // 2
    FF = ffn_gate.shape[2]
    FN = FF // P
    NM = w_ada.shape[2] // P
    NE = router_w.shape[2]
    FE = moe_gate.shape[3]
    EPS = 1e-6
    LAT = slice(S, T)
    ALL = slice(0, T)
    assert (S, D, L, DS, G, NS, GH, FN) == (256, 1024, 2, 512, 32, 64, 16, 22) and FE == FF

    with ExitStack() as stack:
        sems = {}

        def sem(name):
            if name not in sems:
                sems[name] = stack.enter_context(nc.semaphore(name))
            return sems[name]

        def sb(name, shape, dt=F32):
            return stack.enter_context(nc.sbuf_tensor(name, shape, dt))

        hT = sb("hT", [P, KC, T])
        aT = sb("aT", [P, KC, T])
        SLOT = KC * 512
        ring = sb("ring", [P, 4 * SLOT])
        WORK = 18944
        work = sb("work", [P, WORK])
        apad = sb("apad", [P, MC, 2, S + 2 * PAD])
        ps = stack.enter_context(nc.psum_tensor("ps", [P, 8, 512], F32))

        def view(start, dims, names, rest="", **kw):
            size = 1
            for d in dims:
                size *= d
            return work[:, start:start + size].rearrange(f"p ({names}) -> p {names}", **dict(zip(names.split(), dims)))

        E = view(0, [2, 2, HQ, (CL + 1) * GH], "d r q x")
        Wst = view(4608, [2, 2, HQ, P], "d r q x")
        K = view(8704, [2, 2, 4, P], "f a q x")
        Fq = view(10752, [2, 2, 4, P], "d r q x")
        Pst = view(10752, [2, 2, HQ, NJ], "d r q j")
        R = view(12800, [2, 2, 4, P], "d a q x")
        yt = view(12800, [CL, 256], "t x")
        X = view(14848, [2, 2, HQ, NJ], "d r q j")
        T1 = view(14848, [G, 4, GH], "g i h")
        U = view(16896, [G, NJ], "g j")
        GO = view(16896, [MC, T], "m t")
        Braw = view(16896, [2, 2, Q * GH], "r d x")
        Craw = view(17920, [2, 4, P], "r d x")
        yE = view(0, [KC, T], "k t")
        rows_v = work[0:112, 12800:12928]
        rows_b = work[0:L * NM, 12928:13056]
        rows_z = work[0:64, 13056:13568].rearrange("p (k x) -> p k x", k=4)
        rows_w = work[0:L * CW, 13568:14080]
        rows_d = work[0:G, 14080:14336].rearrange("p (l s h) -> p l s h", l=L, s=CL)
        load_d = work[0:G, 14336:14368].rearrange("p (l h) -> p l h", l=L)
        load_dt = work[0:64, 14368:14370]
        dt = work[0:64, 14370:14372]
        zl = work[:, 4608:4864].rearrange("p (k x) -> p k x", k=4)
        dz = work[:, 4864:5760].rearrange("p (k x) -> p k x", k=14)
        hid = view(0, [FN, T], "f t")
        xg = view(0, [NE, KC, P], "e k s")
        Gt = view(8192, [NE, S], "e t")
        acc = view(10240, [KC, S], "k t")
        ysb = view(12288, [D], "n")

        ident = sb("ident", [P, P])
        ones = sb("ones", [P, P])
        iota_s = sb("iota_s", [P, P])
        before = sb("before", [P, P])
        eyeh = sb("eyeh", [P, GH])
        eps_t = sb("eps_t", [P, 1])
        vT = sb("vT", [P, 112])
        bT = sb("bT", [P, L * NM])
        cwT = sb("cwT", [P, MC, L * CW])
        dT = sb("dT", [P, L, G])
        spare = ring[:, 3 * SLOT:4 * SLOT]
        pw = spare[:, 0:1152].rearrange("p (r l d q s) -> p r l d q s", r=2, l=L, d=2, q=Q)
        aw = sb("aw", [P, 2, L, 2, Q, NB])
        pc = sb("pc", [P, 4, 64])
        a1 = sb("a1", [P, 2, 64])
        a1s = sb("a1s", [P, 2, 64])
        a8 = sb("a8", [P, 2, 64])
        a8s = sb("a8s", [P, 2, 64])
        cf = sb("cf", [P, 2, 64])
        Bb = spare[:, 1152:2176].rearrange("p (r d q h) -> p r d q h", r=2, d=2, q=Q)
        Ct = spare[:, 2176:3200].rearrange("p (r d q h) -> p r d q h", r=2, d=2, q=Q)
        modT = sb("modT", [P, L, NM, 2])
        amp = sb("amp", [P, L, 4, KC, 2])
        sc = sb("sc", [P, KC, 2])
        sq = sb("sq", [P, 2, T])
        std = sb("std", [P, T])
        rstd = sb("rstd", [P, T])
        sg = sb("sg", [P, 2, T])
        gcar = std[:, 0:256].rearrange("p (d r q b) -> p d r q b", d=2, r=2, q=HQ)
        gpre = std[:, 256:512].rearrange("p (d r q b) -> p d r q b", d=2, r=2, q=HQ)
        tS = sg[:, 0, :].rearrange("p (d i r x) -> p d i r x", d=2, i=2, r=2)
        dg = sb("dg", [P, 4, P])
        wr = sb("wr", [P, KC, NE])
        br = sb("br", [1, NE])
        lg = sb("lg", [P, 2, NE])
        top = sb("top", [P, 2, 8])
        topi = sb("topi", [P, 2, 8], U32)
        topf = sb("topf", [P, 2, 8])
        hot = sb("hot", [P, 2, 2, NE])
        gw = sb("gw", [P, 2, 4])
        gate = sb("gate", [P, 2, NE])
        mask = sb("mask", [P, 2, NE])
        slot_of = sb("slot_of", [P, 2, NE])
        most = sb("most", [P, 1])
        most_i = sb("most_i", [P, 1], I32)
        tick = sb("tick", [P, 1])

        xin = aT[:, :, :].rearrange("p k t -> p (k t)").rearrange("p (i n) -> p i n", i=4)

        def slot(n):
            return ring[:, (n % 3) * SLOT:(n % 3 + 1) * SLOT]

        def cols(w, a, b, at=0):
            return at, w.shape[0] // P, b - a, w[:, a:b].rearrange("(k p) n -> p k n", p=P)

        ADA = NM // 4
        steps = [[cols(w_ada[l], 512 * i, 512 * i + 512)] for l in range(L) for i in range(ADA)]
        N_ADA = len(steps)
        at = {}
        for l in range(L):
            at["in", l] = len(steps)
            steps += [[cols(w_in[l], 512 * i, 512 * i + 512)] for i in range(3)]
            at["glu", l] = len(steps)
            steps += [[cols(w_glu[l], 0, DS)]]
            at["out", l] = len(steps)
            steps += [[cols(w_out[l], 512 * i, 512 * i + 512)] for i in range(2)]
            if l == 0:
                at["ffn"] = len(steps)
                steps += [[cols(ffn_gate[0], 256 * i, 256 * i + 256), cols(ffn_up[0], 256 * i, 256 * i + 256, 2048)]
                          for i in range(FN // 2)]
                at["down"] = len(steps)
                steps += [[cols(ffn_down[0], P * i, P * i + P)] for i in range(KC)]
        landed = []
        per_slot = [0, 0, 0]
        for n, s in enumerate(steps):
            per_slot[n % 3] += 16 * len(s)
            landed.append(per_slot[n % 3])

        def weights(n, i=0):
            a, k, w, _ = steps[n][i]
            return slot(n)[:, a:a + k * w].rearrange("p (k w) -> p k w", k=k)

        def norm_cols(n):
            return LAT if n > 4 else ALL

        def streams(cs):
            return [(1, LAT)] if cs == LAT else [(0, slice(0, S)), (1, LAT)]

        GU = [ring[:, 4096 * i:4096 * (i + 1)].rearrange("p (a k f) -> p a k f", a=2, k=KC) for i in range(4)]
        DN = [None] * 3
        Sel = view(12800 + 512, [2, NE, P], "i e s")
        DN[0] = work[:, 13312:15360].rearrange("p (f n) -> p f n", f=2)
        Sg = view(15360, [2, NE, P], "i e s")
        DN[1] = work[:, 15360:17408].rearrange("p (f n) -> p f n", f=2)
        ftok = apad[:, :, :, :].rearrange("p m i t -> p (m i t)")[:, 0:2 * D].rearrange("p (i n) -> p i n", i=2)
        DN[2] = apad[:, :, :, :].rearrange("p m i t -> p (m i t)")[:, 0:2 * D].rearrange("p (f n) -> p f n", f=2)
        hide = work[:, 17408:17920].rearrange("p (b f s) -> p b f s", b=2, f=2)
        sge = work[:, 17920:18432].rearrange("p (b n) -> p b n", b=2)
        NSTEP = FE // 256
        USES = [3, 3, 3, 2]
        DUSES = [4, 4, 3]

        block = stack.enter_context(nc.Block())

        @block.sync
        def _(sp):
            def load(n):
                if n >= 3:
                    sp.wait_ge(sem("step_used"), n - 2)
                for i, (_, _, _, src) in enumerate(steps[n]):
                    sp.dma_start(weights(n, i), src).then_inc(sem(f"ring_in{n % 3}"), 16)

            for i, src in enumerate((ctx_in, x)):
                sp.dma_start(xin[:, 2 * i:2 * i + 2, :], src[0].rearrange("(i p) n -> p i n", p=P)).then_inc(sem("x_in"), 16)
            for n in range(3):
                load(n)
            for l in range(L):
                src = w_ada[l].rearrange("(k p) n -> p k n", p=P)
                with sp.Fori(1 if l == 0 else 0, ADA // 3) as it:
                    for s in range(3):
                        sp.wait_ge(sem("step_used"), 3 * it + (l * ADA + s - 2))
                        sp.dma_start(weights(s), src[:, :, bass.ds(it * 1536 + 512 * s, 512)]).then_inc(sem(f"ring_in{s}"), 16)
            for n in range(N_ADA, len(steps)):
                load(n)

            def load_gu(e, c):
                for i, w in enumerate((moe_gate, moe_up)):
                    sp.dma_start(GU[c % 4][:, i], w[0, e, :, 256 * c:256 * c + 256].rearrange("(k p) n -> p k n", p=P))\
                        .then_inc(sem(f"gu_in{c % 4}"), 16)

            def load_dn(e, c):
                sp.dma_start(DN[c % 3], moe_down[0, e, 256 * c:256 * c + 256, :].rearrange("(f p) n -> p f n", p=P))\
                    .then_inc(sem(f"dn_in{c % 3}"), 16)

            def experts(ph):
                g0 = ph * NE * NSTEP
                if ph:
                    sp.wait_ge(sem("dn_done"), g0)
                else:
                    sp.wait_ge(sem("step_used"), len(steps))
                for c in range(4):
                    load_gu(0, c)
                sp.wait_ge(sem("moved"), 20 * (ph + 1))
                for c in range(3):
                    load_dn(0, c)

                def body(e, last):
                    for c in range(NSTEP):
                        if c + 4 < NSTEP or not last:
                            after = c if c + 4 < NSTEP else (8, 9, 10, 7)[c + 4 - NSTEP]
                            sp.wait_ge(sem("gu_done"), e * NSTEP + (g0 + after + 1))
                            load_gu(e if c + 4 < NSTEP else e + 1, (c + 4) % NSTEP)
                        if c >= 1 and (c + 2 < NSTEP or not last):
                            after = c - 1 if c + 2 < NSTEP else (9, 10)[c + 2 - NSTEP]
                            sp.wait_ge(sem("dn_done"), e * NSTEP + (g0 + after + 1))
                            load_dn(e if c + 2 < NSTEP else e + 1, (c + 2) % NSTEP)
                    if not last:
                        load_dn(e + 1, 2)

                with sp.Fori(0, NE - 1) as e:
                    body(e, False)
                body(NE - 1, True)

            experts(0)
            sp.wait_ge(sem("routed"), 1)
            over = sp.value_load(most_i[0:1, 0:1], min_val=0, max_val=S)
            with sp.If(over > P):
                experts(1)
            sp.wait_ge(sem("rows_out"), 2)
            for i in range(2):
                sp.dma_start(out[0, i * P:(i + 1) * P, :], hT[:, 4 * i:4 * i + 4, 0:S]).then_inc(sem("out_done"), 16)
            sp.wait_ge(sem("out_done"), 32)

        @block.gpsimd
        def _(pool):
            n = sem("consts")
            pool.memset(ident[:], 0.0).then_inc(n, 1)
            pool.memset(ones[:], 1.0).then_inc(n, 1)
            pool.memset(eps_t[:], EPS).then_inc(n, 1)
            pool.memset(apad[:], 0.0).then_inc(n, 1)
            pool.iota(iota_s[:], pattern=[[1, P]], base=0, channel_multiplier=0,
                      allow_small_or_imprecise_dtypes=True).then_inc(n, 1)
            pool.wait_ge(n, 5)
            pool.affine_select(out=ident[:], in_=ident[:], compare_op=ALU.not_equal, fill=1.0, base=0,
                               pattern=[[-1, P]], channel_multiplier=1).then_inc(n, 1)
            pool.affine_select(out=before[:], in_=ones[:], compare_op=ALU.is_gt, fill=0.0, base=0,
                               pattern=[[1, P]], channel_multiplier=-1).then_inc(n, 1)
            pool.wait_ge(n, 7)
            pool.wait_ge(sem("par"), 5)
            i = 0
            for l in range(L):
                for m in range(MC):
                    for k in range(CW):
                        if i >= 4:
                            pool.wait_ge(sem("tap_used"), i - 3)
                        pool.tensor_scalar(dg[:, i % 4, :], ident[:], cwT[:, m, l * CW + k:l * CW + k + 1], 0.0,
                                           ALU.mult, ALU.add).then_inc(sem("tap"), 1)
                        i += 1

        @block.scalar
        def _(act):
            r = sem("rows_in")
            row = 0
            for w in (g_pre_mix, g_post_mix, g_pre_ffn, g_post_ffn, b_glu, conv_b, ln_g, ln_b):
                k = L * w.shape[1] // P
                act.dma_start(rows_v[row:row + k], w.rearrange("l (c p) -> (l c) p", p=P)).then_inc(r, 16)
                row += k
            act.dma_start(rows_v[row:row + KC], c_ctx.rearrange("(c p) -> c p", p=P)).then_inc(r, 16)
            act.dma_start(rows_v[row + KC:row + 2 * KC], c[0].rearrange("(c p) -> c p", p=P)).then_inc(r, 16)
            act.dma_start(rows_b, b_ada.rearrange("l (c p) -> (l c) p", p=P)).then_inc(r, 16)
            act.dma_start(rows_w, conv_w.rearrange("l k n -> (l k) n")).then_inc(r, 16)
            act.dma_start(rows_z[:, 2], lam_re.rearrange("l d (q a) p -> (l d q) (a p)", a=2)).then_inc(r, 16)
            act.dma_start(rows_z[:, 3], lam_im.rearrange("l d (q a) p -> (l d q) (a p)", a=2)).then_inc(r, 16)
            act.dma_start(load_dt, log_dt.rearrange("l d (q a) -> (l d q) a", a=2)).then_inc(r, 16)
            act.dma_start(load_d, ssm_d.rearrange("l (g h) -> g l h", h=GH)).then_inc(r, 16)

            def load_bc(l):
                for i, w in enumerate((b_re, b_im)):
                    for d in range(2):
                        for a in range(2):
                            act.dma_start(Braw[HP * a:HP * a + HP, i, d].rearrange("p (q h) -> p q h", h=GH),
                                          w[l, d].rearrange("(q a) p h -> a p q h", a=2)[a]).then_inc(sem("bc_in"), 16)
                for i, w in enumerate((c_re, c_im)):
                    for q in range(HQ):
                        src = w[l].rearrange("d (f q a) h p -> q a h (d f) p", f=2, a=2)[q]
                        for a in range(2):
                            act.dma_start(Craw[GH * q:GH * q + GH, i, :, HP * a:HP * a + HP], src[a])\
                                .then_inc(sem("bc_in"), 16)

            load_bc(0)
            act.dma_start(wr[:], router_w[0].rearrange("(k p) e -> p k e", p=P)).then_inc(sem("router_in"), 16)
            act.dma_start(br[:], router_b).then_inc(sem("router_in"), 16)
            act.wait_ge(r, 16 * 16)
            act.activation(dt, load_dt, ACT.Exp).then_inc(sem("dt"), 1)

            for k in range(KC):
                act.wait_ge(sem("x_turned"), k + 1)
                act.activation(hT[:, k, :], ps[:, 3 + k % 4, :], ACT.Copy).then_inc(sem("x_copied"), 1)
            act.wait_ge(sem("angle"), 1)
            act.activation(dz[:, 2], zl[:, 0], ACT.Exp).then_inc(sem("polar"), 1)
            act.activation(dz[:, 3], dz[:, 0], ACT.Sin).then_inc(sem("polar"), 1)
            act.activation(dz[:, 4], dz[:, 1], ACT.Sin).then_inc(sem("polar"), 1)
            act.wait_ge(sem("par"), 5)
            act.activation(sc[:].rearrange("p k s -> p s k"), vT[:, 96:112].rearrange("p (s k) -> p s k", s=2),
                           ACT.Silu).then_inc(sem("silu_c"), 1)

            def prep(l, h):
                for qq in range(2):
                    n = 4 * l + 2 * h + qq
                    for i in range(4):
                        act.wait_ge(sem("w_turned"), 4 * n + i + 1)
                        act.activation(Wst[:, i // 2, i % 2, 4 * qq:4 * qq + 4, :],
                                       ps[:, i, :].rearrange("p (q x) -> p q x", q=4), ACT.Copy).then_inc(sem("w_copied"), 1)
                    for i in range(4):
                        d, r_ = i // 2, i % 2
                        b = Bb[:, r_, d, HQ * h + 4 * qq:HQ * h + 4 * qq + 4, :].rearrange("p q (s h) -> p q s h", s=1)
                        act.activation(Fq[:, d, r_].rearrange("p q (s h) -> p q s h", h=GH), b.broadcast_to([P, 4, CL, GH]),
                                       ACT.Copy).then_inc(sem("b_spread"), 1)
                    act.wait_ge(sem("r_ready"), n + 1)
                    if 2 * l + h:
                        act.wait_ge(sem("y_chunks"), 4 * (2 * l + h))
                    for s in range(CL):
                        row = slice(GH * s, GH * s + GH)
                        act.dma_start(K[row, qq, :, :, GH * s:P].rearrange("p a q x -> p (a q) x"),
                                      R[row, 0, :, :, 0:P - GH * s].rearrange("p a q x -> p (a q) x")).then_inc(sem("k_in"), 16)
                        if s:
                            act.dma_start(K[row, qq, :, :, 0:GH * s].rearrange("p a q x -> p (a q) x"),
                                          R[row, 1, :, :, P - GH - GH * s:P - GH].rearrange("p a q x -> p (a q) x")).then_inc(sem("k_in"), 16)

            def norm(n, src, ready):
                cs = norm_cols(n)
                for k in range(KC):
                    i = KC * n + k
                    ready(k)
                    if i >= 2:
                        act.wait_ge(sem("sq_used"), i - 1)
                    act.activation(sq[:, i % 2, cs], src(k), ACT.Square).then_inc(sem("sq_ready"), 1)
                act.wait_ge(sem("sq_used"), KC * n + KC)
                act.activation(std[:, cs], ps[:, 6, cs], ACT.Sqrt, bias=eps_t[:, 0:1], scale=1.0 / D)\
                    .then_inc(sem("std_ready"), 1)

            def shift(n):
                l, i = n // 4, 3 * (n % 4 // 2)
                for k in range(KC):
                    for j, (s, cols_) in enumerate(streams(norm_cols(n))):
                        act.wait_ge(sem(f"scaled{n}"), k * len(streams(norm_cols(n))) + j + 1)
                        act.activation(aT[:, k, cols_], aT[:, k, cols_], ACT.Identity,
                                       bias=modT[:, l, KC * i + k, s:s + 1]).then_inc(sem(f"a_ready{n}"), 1)

            prep(0, 0)
            for l in range(L):
                lat = LAT if l else ALL
                n0 = 4 * l
                norm(n0, lambda k: hT[:, k, norm_cols(n0)],
                     (lambda k: None) if l == 0 else (lambda k: act.wait_ge(sem("h_ready3"), k + 1)))
                shift(n0)
                for i in range(4):
                    act.wait_ge(sem(f"u_done{l}"), i + 1)
                    act.activation(T1[:, :, i, :], ps[:, i, :].rearrange("p (g h) -> p g h", h=GH), ACT.Copy).then_inc(sem(f"t1_copied{l}"), 1)
                for m in range(MC):
                    act.wait_ge(sem(f"vg_done{l}"), m + 1)
                    if m >= 2:
                        act.wait_ge(sem(f"gated{l}"), m - 1)
                    act.activation(sg[:, m % 2, lat], ps[:, 5 + 2 * (m % 2), lat], ACT.Sigmoid).then_inc(sem(f"vg_sig{l}"), 1)
                for h in range(2):
                    if 2 * l + h:
                        if h == 0:
                            act.wait_ge(sem("w_out_done0"), KC)
                            load_bc(1)
                        prep(l, h)
                    for i in range(4):
                        act.wait_ge(sem("x_done"), 4 * (2 * l + h) + i + 1)
                        act.activation(X[:, i // 2, i % 2], ps[:, i, :].rearrange("p (q j) -> p q j", q=HQ), ACT.Copy)\
                            .then_inc(sem("x_states"), 1)
                    for m in (2 * h, 2 * h + 1):
                        act.wait_ge(sem(f"conv_done{l}"), m + 1) if m % 2 == 0 else None
                        if m % 2 == 0:
                            act.activation(aT[:, MC + m, lat], ps[:, 7, lat], ACT.Identity,
                                           bias=vT[:, 72 + MC * l + m:73 + MC * l + m]).then_inc(sem(f"conv_copied{l}"), 1)
                    for i in range(4):
                        act.wait_ge(sem("y_chunks"), 4 * (2 * l + h) + i + 1)
                        g2, b = i // 2, i % 2
                        dst = yt[0:NJ].rearrange("p t (q a h) -> p a q t h", a=2, h=GH)[:, g2, 4 * b:4 * b + 4]
                        act.activation(dst, ps[0:NJ, i, :].rearrange("p (q t h) -> p q t h", q=4, h=GH), ACT.Copy)\
                            .then_inc(sem("yt_copied"), 1)
                    for i in range(2):
                        act.wait_ge(sem("z_turned"), 2 * (2 * l + h) + i + 1)
                        act.activation(aT[:, 2 * h + i, :].rearrange("p (j t) -> p j t", t=CL),
                                       ps[:, 4 + i, :].rearrange("p (t j) -> p j t", t=CL), ACT.Gelu_apprx_tanh)\
                            .then_inc(sem(f"z_ready{l}"), 1)
                    m = 2 * h + 1
                    act.wait_ge(sem(f"conv_done{l}"), m + 1)
                    act.activation(aT[:, MC + m, lat], ps[:, 7, lat], ACT.Identity,
                                   bias=vT[:, 72 + MC * l + m:73 + MC * l + m]).then_inc(sem(f"conv_copied{l}"), 1)
                for m in range(MC):
                    act.wait_ge(sem(f"glu_done{l}"), m + 1)
                    if m >= 2:
                        act.wait_ge(sem(f"glu_used{l}"), m - 1)
                    act.activation(sg[:, m % 2, lat], ps[:, m, lat], ACT.Sigmoid,
                                   bias=vT[:, 64 + MC * l + m:65 + MC * l + m]).then_inc(sem(f"glu_sig{l}"), 1)
                for m in range(MC):
                    act.wait_ge(sem(f"centred{l}"), m + 1)
                    if m >= 2:
                        act.wait_ge(sem(f"ln_used{l}"), m - 1)
                    act.activation(sq[:, m % 2, lat], aT[:, MC + m, lat], ACT.Square).then_inc(sem(f"ln_sq{l}"), 1)
                act.wait_ge(sem(f"ln_used{l}"), MC)
                act.activation(std[:, lat], ps[:, 6, lat], ACT.Sqrt, bias=eps_t[:, 0:1], scale=1.0 / DS)\
                    .then_inc(sem(f"ln_std{l}"), 1)
                for m in range(MC):
                    act.wait_ge(sem(f"ln_scaled{l}"), m + 1)
                    act.activation(aT[:, MC + m, lat], aT[:, MC + m, lat], ACT.Silu,
                                   scale=vT[:, 80 + MC * l + m:81 + MC * l + m],
                                   bias=vT[:, 88 + MC * l + m:89 + MC * l + m]).then_inc(sem(f"cv_ready{l}"), 1)
                norm(n0 + 1, lambda k: yE[:, k, lat], lambda k: act.wait_ge(sem(f"y_copied{n0 + 1}"), k + 1))
                norm(n0 + 2, lambda k: hT[:, k, lat], lambda k: act.wait_ge(sem(f"h_ready{n0 + 1}"), k + 1))
                shift(n0 + 2)
                if l == 0:
                    for i in range(FN):
                        act.wait_ge(sem("ffn_done"), i + 1)
                        if i >= 2:
                            act.wait_ge(sem("hid_ready"), i - 1)
                        act.activation(sg[:, i % 2, :], ps[:, 2 * (i % 3), :], ACT.Silu).then_inc(sem("ffn_silu"), 1)
                    norm(3, lambda k: aT[:, k, :], lambda k: act.wait_ge(sem("y_copied3"), k + 1))

            act.wait_ge(sem("top2"), 1)
            act.activation(gw[:, :, 1:2], gw[:, :, 0:1], ACT.Exp).then_inc(sem("gate_exp"), 1)

            def experts(ph):
                for i in range(16):
                    act.wait_ge(sem("gathered"), 16 * ph + i + 1)
                    act.activation(xg[:, 4 * (i % 2):4 * (i % 2) + 4, i // 2, :],
                                   ps[:, i % 4, :].rearrange("p (e s) -> p e s", e=4), ACT.Copy).then_inc(sem("moved"), 1)
                for i in range(4):
                    act.wait_ge(sem("gates_turned"), 4 * ph + i + 1)
                    act.activation(Gt[:, 4 * (i % 2):4 * (i % 2) + 4, P * (i // 2):P * (i // 2) + P],
                                   ps[:, 4 + i, :].rearrange("p (e s) -> p e s", e=4), ACT.Copy).then_inc(sem("moved"), 1)
                with act.Fori(0, NE) as e:
                    for c_ in range(NSTEP):
                        g = ph * NE * NSTEP + c_
                        act.wait_ge(sem("gu_done"), e * NSTEP + (g + 1))
                        if c_ >= 2:
                            act.wait_ge(sem("hide_ready"), e * NSTEP + (g - 1))
                        act.activation(sge[:, c_ % 2, :], ps[:, c_ % 2, 0:256], ACT.Silu).then_inc(sem("sge_ready"), 1)
                    act.wait_ge(sem("dn_done"), e * NSTEP + (ph * NE * NSTEP + NSTEP))
                    act.activation(ysb[:, 0:512], ps[:, 2, :], ACT.Copy).then_inc(sem("ysb_ready"), 1)

            experts(0)
            act.wait_ge(sem("routed"), 1)
            over = act.value_load(most_i[0:1, 0:1], min_val=0, max_val=S)
            with act.If(over > P):
                experts(1)
            norm(7, lambda k: acc[:, k, :], lambda k: act.wait_ge(sem("summed"), 1))

        @block.tensor
        def _(pe):
            def mm(o, lhs, rhs, start=True, stop=True):
                return pe.matmul(o, lhs, rhs, start=start, stop=stop)

            def turn(o, i, n=P):
                return pe.transpose(o, i, ident[0:n, 0:n])

            def step_in(n):
                pe.wait_ge(sem(f"ring_in{n % 3}"), landed[n])

            pe.wait_ge(sem("consts"), 7)
            pe.wait_ge(sem("rows_in"), 16 * 16)
            turn(ps[:, 0, 0:112], rows_v, 112)
            turn(ps[:, 0, 128:128 + L * NM], rows_b, L * NM)
            for m in range(MC):
                turn(ps[:, 1, L * CW * m:L * CW * (m + 1)], rows_w[:, P * m:P * m + P], L * CW)
            pe.wait_ge(sem("z_rows"), 5)
            for l in range(L):
                turn(ps[:, 1, 256 + G * l:256 + G * l + G], rows_d[:, l].rearrange("p s h -> p (s h)"), G)
            for i in range(4):
                last = turn(ps[:, 2, 64 * i:64 * i + 64], rows_z[:, i, :], 64)
            last.then_inc(sem("rows_turned"), 1)
            pe.wait_ge(sem("x_in"), 32)
            for k in range(KC):
                if k >= 4:
                    pe.wait_ge(sem("x_copied"), k - 3)
                for i in range(4):
                    last = turn(ps[:, 3 + k % 4, P * i:P * i + P], xin[:, i, P * k:P * k + P])
                last.then_inc(sem("x_turned"), 1)

            def turn_c(l):
                pe.wait_ge(sem("bc_in"), 16 * 40 * (l + 1))
                if l == 0:
                    pe.wait_ge(sem("par"), 5)
                for i in range(2):
                    for j in range(4):
                        last = turn(ps[:, i, P * j:P * j + P], Craw[:, i, j, :])
                    last.then_inc(sem("c_turned"), 1)

            def prep(l, h):
                for qq in range(2):
                    n = 4 * l + 2 * h + qq
                    if qq == 0 and h:
                        pe.wait_ge(sem(f"z_ready{l}"), 2)
                        pe.wait_ge(sem(f"conv_copied{l}"), 2)
                    elif qq == 0 and l:
                        pe.wait_ge(sem("t1_copied1"), 4)
                        pe.wait_ge(sem("gated1"), MC)
                    pe.wait_ge(sem("f_ready"), n + 1)
                    if n:
                        pe.wait_ge(sem("w_copied"), 4 * n)
                    else:
                        pe.wait_ge(sem("x_copied"), KC)
                    if qq == 0 and h == 0:
                        pe.wait_ge(sem("c_copied"), 2 * (l + 1))
                    for i in range(4):
                        for q in range(4):
                            last = turn(ps[:, i, P * q:P * q + P], Fq[:, i // 2, i % 2, q, :])
                        last.then_inc(sem("w_turned"), 1)
                    if n:
                        pe.wait_ge(sem("r_copied"), 4 * n)
                    pe.wait_ge(sem("b_spread"), 4 * (n + 1))
                    for d in range(2):
                        for a in range(2):
                            rows = slice(HP * a, HP * a + HP)
                            for q in range(4):
                                for r in range(2):
                                    last = mm(ps[:, 4 + 2 * d + a, P * q:P * q + P], Fq[rows, d, r, q, :],
                                              E[rows, d, r, 4 * qq + q, GH * d:GH * d + P], start=r == 0, stop=r == 1)
                            last.then_inc(sem("r_done"), 1)

            turn_c(0)
            prep(0, 0)
            pe.wait_ge(sem("silu_c"), 1)
            pe.wait_ge(sem("r_copied"), 8)
            mod_ps = ps[:, 7, 0:2 * L * NM]
            with pe.Fori(0, N_ADA // 3) as it:
                for s in range(3):
                    pe.wait_ge(sem(f"ring_in{s}"), it * 16 + 16)
                    w = weights(s)
                    for m in range(4):
                        for k in range(KC):
                            last = mm(mod_ps[:, bass.ds(it * 24 + (8 * s + 2 * m), 2)], w[:, k, P * m:P * m + P], sc[:, k, :],
                                      start=k == 0, stop=k == KC - 1)
                    last.then_inc(sem("step_used"), 1)

            def norm(n):
                cs = norm_cols(n)
                for k in range(KC):
                    pe.wait_ge(sem("sq_ready"), KC * n + k + 1)
                    mm(ps[:, 6, cs], ones[:], sq[:, (KC * n + k) % 2, cs], k == 0, k == KC - 1).then_inc(sem("sq_used"), 1)

            def conv(l, m):
                lat = slice(1, 2) if l else slice(0, 2)
                if m == 0:
                    pe.wait_ge(sem(f"gated{l}"), MC)
                if m % 2 == 0:
                    pe.wait_ge(sem("r_copied"), 8 * (2 * l + m // 2 + 1))
                if m >= 1:
                    pe.wait_ge(sem(f"conv_copied{l}"), m)
                o = ps[:, 7, LAT if l else ALL].rearrange("p (i t) -> p i t", t=S)
                for k in range(CW):
                    i = (l * MC + m) * CW + k
                    pe.wait_ge(sem("tap"), i + 1)
                    last = mm(o, dg[:, i % 4, :], apad[:, m, lat, k:k + S], k == 0, k == CW - 1)
                    last.then_inc(sem("tap_used"), 1)
                pe.wait_ge(sem("tap_used"), (l * MC + m + 1) * CW)
                pe.sem_inc(sem(f"conv_done{l}"), 1)

            def project(n, w_at, width, rhs, nk, cs):
                for m in range(KC):
                    if m * P % width == 0:
                        step_in(w_at + m * P // width)
                    if m >= 4:
                        pe.wait_ge(sem(f"y_copied{n}"), m - 3)
                    w = weights(w_at + m * P // width)
                    for k in range(nk):
                        last = mm(ps[:, m % 4, cs], w[:, k, m * P % width:m * P % width + P], rhs(k), k == 0, k == nk - 1)
                    last.then_inc(sem(f"y_done{n}"), 1)
                    if (m + 1) * P % width == 0:
                        pe.wait_ge(sem(f"y_done{n}"), m + 1)
                        pe.sem_inc(sem("step_used"), 1)

            for l in range(L):
                lat = LAT if l else ALL
                n0 = 4 * l
                if l == 0:
                    pe.wait_ge(sem("x_copied"), KC)
                norm(n0)
                pe.wait_ge(sem(f"a_ready{n0}"), 2 * KC)
                n_in = at["in", l]
                step_in(n_in)
                w = weights(n_in)
                for i in range(4):
                    for k in range(KC):
                        last = mm(ps[:, i, :], aT[:, k, i:T:4], w[:, k, :], k == 0, k == KC - 1)
                    last.then_inc(sem(f"u_done{l}"), 1)
                pe.wait_ge(sem(f"u_done{l}"), 4)
                pe.sem_inc(sem("step_used"), 1)
                step_in(n_in + 1)
                step_in(n_in + 2)
                for m in range(MC):
                    if m >= 2:
                        pe.wait_ge(sem(f"gated{l}"), m - 1)
                    for i in range(2):
                        w = weights(n_in + 1 + i)
                        for k in range(KC):
                            last = mm(ps[:, 4 + i + 2 * (m % 2), lat], w[:, k, P * m:P * m + P], aT[:, k, lat], k == 0, k == KC - 1)
                    last.then_inc(sem(f"vg_done{l}"), 1)
                pe.wait_ge(sem(f"vg_done{l}"), MC)
                pe.sem_inc(sem("step_used"), 2)
                if l:
                    turn_c(1)
                    prep(1, 0)
                pe.wait_ge(sem(f"t1_copied{l}"), 4)
                if l:
                    pe.wait_ge(sem("w_copied"), 4 * 6)
                    pe.wait_ge(sem("bb_ready"), 2)
                for i in range(8):
                    if i >= 4:
                        pe.wait_ge(sem(f"u_copied{l}"), i - 3)
                    for g in range(4):
                        last = turn(ps[0:HP, i % 4, P * g:P * g + P], T1[:, 4 * i + g].rearrange("p i h -> p (i h)"))
                    last.then_inc(sem(f"u_turned{l}"), 1)
                for h in range(2):
                    hh = 2 * l + h
                    if h:
                        prep(l, 1)
                    pe.wait_ge(sem(f"u_copied{l}"), 8)
                    pe.wait_ge(sem("w_copied"), 8 * (hh + 1))
                    for i in range(4):
                        for q in range(HQ):
                            for a in range(2):
                                last = mm(ps[HP * a:HP * a + HP, i, NJ * q:NJ * q + NJ],
                                          Wst[:, i // 2, i % 2, q, HP * a:HP * a + HP], U[:, 2 * (HQ * h + q) + a, :])
                        last.then_inc(sem("x_done"), 1)
                    conv(l, 2 * h)
                    pe.wait_ge(sem("k_in"), 16 * 15 * 2 * (hh + 1))
                    pe.wait_ge(sem("p_ready"), hh + 1)
                    for i in range(4):
                        a, b = i // 2, i % 2
                        rows = slice(HP * a, HP * a + HP)
                        for qi in range(4):
                            q = 4 * b + qi
                            o = ps[0:NJ, i, P * qi:P * qi + P]
                            mm(o, U[:, 2 * (HQ * h + q) + a, :], K[:, b, a, qi, :], True, False)
                            for d in range(2):
                                for r in range(2):
                                    lo = GH * (1 - d)
                                    last = mm(o, Pst[rows, d, r, q, :], E[rows, d, r, q, lo:lo + P], False, d == 1 and r == 1)
                        last.then_inc(sem("y_chunks"), 1)
                    pe.wait_ge(sem("yt_copied"), 4 * (hh + 1))
                    for i in range(2):
                        for t in range(CL):
                            last = turn(ps[:, 4 + i, NJ * t:NJ * t + NJ], yt[0:NJ, t, P * i:P * i + P], NJ)
                        last.then_inc(sem("z_turned"), 1)
                    conv(l, 2 * h + 1)
                pe.wait_ge(sem(f"z_ready{l}"), MC)
                step_in(at["glu", l])
                w = weights(at["glu", l])
                for m in range(MC):
                    for k in range(MC):
                        last = mm(ps[:, m, lat], w[:, k, P * m:P * m + P], aT[:, k, lat], k == 0, k == MC - 1)
                    last.then_inc(sem(f"glu_done{l}"), 1)
                pe.wait_ge(sem(f"glu_done{l}"), MC)
                pe.sem_inc(sem("step_used"), 1)
                pe.wait_ge(sem(f"conv_copied{l}"), MC)
                for m in range(MC):
                    last = mm(ps[:, 5, lat], ones[:], aT[:, MC + m, lat], m == 0, m == MC - 1)
                last.then_inc(sem(f"ln_sum{l}"), 1)
                for m in range(MC):
                    pe.wait_ge(sem(f"ln_sq{l}"), m + 1)
                    mm(ps[:, 6, lat], ones[:], sq[:, m % 2, lat], m == 0, m == MC - 1).then_inc(sem(f"ln_used{l}"), 1)
                pe.wait_ge(sem(f"go_ready{l}"), MC)
                pe.wait_ge(sem(f"cv_ready{l}"), MC)
                project(n0 + 1, at["out", l], 512, lambda k: GO[:, k, lat] if k < MC else aT[:, k, lat], KC, lat)
                pe.wait_ge(sem(f"y_done{n0 + 1}"), KC)
                pe.sem_inc(sem(f"w_out_done{l}"), KC)
                norm(n0 + 1)
                norm(n0 + 2)
                pe.wait_ge(sem(f"a_ready{n0 + 2}"), KC * len(streams(lat)))
                if l == 0:
                    for i in range(FN):
                        n = at["ffn"] + i // 2
                        if i % 2 == 0:
                            step_in(n)
                        if i >= 3:
                            pe.wait_ge(sem("hid_ready"), i - 2)
                        for j in range(2):
                            w = weights(n, j)
                            for k in range(KC):
                                last = mm(ps[:, 2 * (i % 3) + j, :], w[:, k, P * (i % 2):P * (i % 2) + P], aT[:, k, :],
                                          k == 0, k == KC - 1)
                        last.then_inc(sem("ffn_done"), 1)
                        if i % 2:
                            pe.wait_ge(sem("ffn_done"), i + 1)
                            pe.sem_inc(sem("step_used"), 1)
                    pe.wait_ge(sem("hid_ready"), FN)
                    project(3, at["down"], P, lambda k: hid[:, k, :], FN, ALL)
                    norm(3)

            for tt in range(2):
                tok = slice(S + P * tt, S + P * tt + P)
                for k in range(KC):
                    mm(ps[:, 4, NE * tt:NE * tt + NE], aT[:, k, tok], wr[:, k, :], k == 0, False)
                if tt == 0:
                    pe.wait_ge(sem("router_in"), 32)
                last = mm(ps[:, 4, NE * tt:NE * tt + NE], ones[0:1, :], br[:], False, True)
            last.then_inc(sem("logits"), 1)
            pe.wait_ge(sem("masked"), 2)
            mm(ps[:, 5, 0:NE], before[:], mask[:, 0], True, True)
            mm(ps[:, 5, NE:2 * NE], before[:], mask[:, 1], True, False)
            mm(ps[:, 5, NE:2 * NE], ones[:], mask[:, 0], False, True)
            mm(ps[:, 5, 2 * NE:3 * NE], ones[:], mask[:, 0], True, False)
            mm(ps[:, 5, 2 * NE:3 * NE], ones[:], mask[:, 1], False, True).then_inc(sem("counted"), 1)

            def experts(ph):
                g0 = ph * NE * NSTEP
                if ph:
                    pe.wait_ge(sem("acc_added"), 4 * NE + 1)
                for i in range(4):
                    for k in range(4):
                        last = turn(ps[:, i, P * k:P * k + P], aT[:, 4 * (i % 2) + k, S + P * (i // 2):S + P * (i // 2) + P])
                    last.then_inc(sem("ftok_turned"), 1)
                pe.wait_ge(sem("ftok_copied"), 4 * (ph + 1))
                pe.wait_ge(sem("selected"), 32 * (ph + 1))
                for i in range(16):
                    if i >= 4:
                        pe.wait_ge(sem("moved"), 20 * ph + i - 3)
                    for tt in range(2):
                        last = mm(ps[:, i % 4, :], ftok[:, tt, P * (i // 2):P * (i // 2) + P],
                                  Sel[:, tt, 4 * (i % 2):4 * (i % 2) + 4, :], tt == 0, tt == 1)
                    last.then_inc(sem("gathered"), 1)
                for i in range(4):
                    for j in range(4):
                        last = turn(ps[:, 4 + i, P * j:P * j + P], Sg[:, i // 2, 4 * (i % 2) + j, :])
                    last.then_inc(sem("gates_turned"), 1)
                pe.wait_ge(sem("moved"), 20 * (ph + 1))

                def down(e, c_):
                    g = g0 + c_
                    pe.wait_ge(sem(f"dn_in{c_ % 3}"), e * (16 * DUSES[c_ % 3]) + 16 * (ph * NE * DUSES[c_ % 3] + c_ // 3 + 1))
                    pe.wait_ge(sem("hide_ready"), e * NSTEP + (g + 1))
                    for f in range(2):
                        for nh in range(2):
                            last = mm(ps[:, 2 + nh, :], hide[:, c_ % 2, f, :], DN[c_ % 3][:, f, 512 * nh:512 * nh + 512],
                                      c_ == 0 and f == 0, c_ == NSTEP - 1 and f == 1)
                    last.then_inc(sem("dn_done"), 1)

                with pe.Fori(0, NE) as e:
                    for c_ in range(NSTEP):
                        g = g0 + c_
                        pe.wait_ge(sem(f"gu_in{c_ % 4}"), e * (32 * USES[c_ % 4]) + 32 * (ph * NE * USES[c_ % 4] + c_ // 4 + 1))
                        if c_ >= 2:
                            pe.wait_ge(sem("hide_ready"), e * NSTEP + (g - 1))
                        for j in range(2):
                            for f in range(2):
                                o = ps[:, c_ % 2, 256 * j + P * f:256 * j + P * f + P]
                                for k in range(KC):
                                    rhs = xg[:, bass.ds(e, 1), k, :].rearrange("p e s -> p (e s)")
                                    last = mm(o, GU[c_ % 4][:, j, k, P * f:P * f + P], rhs, k == 0, k == KC - 1)
                        last.then_inc(sem("gu_done"), 1)
                        if c_:
                            down(e, c_ - 1)
                    down(e, NSTEP - 1)
                    pe.wait_ge(sem("ysb_ready"), e * 2 + (2 * NE * ph + 2))
                    pe.wait_ge(sem("acc_added"), e * 4 + (4 * NE * ph + 1))
                    for k in range(KC):
                        rhs = Gt[:, bass.ds(e, 1), :].rearrange("p e t -> p (e t)")
                        last = mm(ps[:, 4 + k // 2, S * (k % 2):S * (k % 2) + S], ysb[:, P * k:P * k + P], rhs)
                        if k % 2:
                            last.then_inc(sem("spread"), 1)

            experts(0)
            pe.wait_ge(sem("routed"), 1)
            over = pe.value_load(most_i[0:1, 0:1], min_val=0, max_val=S)
            with pe.If(over > P):
                experts(1)
            norm(7)
            for i in range(4):
                for j in range(4):
                    k = 4 * (i % 2) + j
                    pe.wait_ge(sem("h_ready7"), k + 1)
                    last = turn(ps[:, i, P * j:P * j + P], hT[:, k, S + P * (i // 2):S + P * (i // 2) + P])
                last.then_inc(sem("out_turned"), 1)

        @block.vector
        def _(dve):
            count = [0]

            def link(ins):
                count[0] += 1
                ins.then_inc(sem("dve_chain"), 1)
                dve.wait_ge(sem("dve_chain"), count[0])

            tt_, ts_, stt = dve.tensor_tensor, dve.tensor_scalar, dve.scalar_tensor_tensor

            dve.wait_ge(sem("consts"), 7)
            link(dve.tensor_reduce(eyeh[:], ident[:].rearrange("p (s h) -> p h s", h=GH), AX_X, ALU.add))
            dve.wait_ge(sem("rows_in"), 16 * 16)
            dve.wait_ge(sem("dt"), 1)
            for i in range(2):
                for a in range(2):
                    ts_(rows_z[:, i, HP * a:HP * a + HP], rows_z[:, 2 + i, HP * a:HP * a + HP], dt[:, a:a + 1], None,
                        ALU.mult).then_inc(sem("z_rows"), 1)
            dve.tensor_copy(rows_d, load_d.rearrange("p l (s h) -> p l s h", s=1).broadcast_to([G, L, CL, GH]))\
                .then_inc(sem("z_rows"), 1)
            dve.wait_ge(sem("rows_turned"), 1)
            dve.tensor_copy(vT[:], ps[:, 0, 0:112]).then_inc(sem("par"), 1)
            dve.tensor_copy(bT[:], ps[:, 0, 128:128 + L * NM]).then_inc(sem("par"), 1)
            dve.tensor_copy(cwT[:], ps[:, 1, 0:MC * L * CW].rearrange("p (m k) -> p m k", m=MC)).then_inc(sem("par"), 1)
            dve.tensor_copy(dT[:], ps[:, 1, 256:256 + L * G].rearrange("p (l g) -> p l g", l=L)).then_inc(sem("par"), 1)
            dve.tensor_copy(zl, ps[:, 2, 0:256].rearrange("p (k x) -> p k x", k=4)).then_inc(sem("par"), 1)
            dve.wait_ge(sem("par"), 5)
            th = zl[:, 1]
            link(ts_(dz[:, 5], th, 1.0 / TWO_PI, ROUND, ALU.mult, ALU.add))
            link(ts_(dz[:, 5], dz[:, 5], -ROUND, None, ALU.add))
            link(stt(dz[:, 6], dz[:, 5], -TWO_PI_HI, th, ALU.mult, ALU.add))
            link(stt(dz[:, 7], dz[:, 5], -TWO_PI_MID, dz[:, 6], ALU.mult, ALU.add))
            link(stt(dz[:, 6], dz[:, 5], -TWO_PI_LO, dz[:, 7], ALU.mult, ALU.add))
            link(ts_(dz[:, 0], dz[:, 6], -PI, PI, ALU.max, ALU.min))
            link(stt(dz[:, 7], dz[:, 0], -1.0, dz[:, 0], ALU.mult, ALU.max))
            ts_(dz[:, 1], dz[:, 7], -1.0, TWO_PI / 4, ALU.mult, ALU.add).then_inc(sem("angle"), 1)
            lr, li = zl[:, 2], zl[:, 3]
            link(tt_(dz[:, 8], lr, lr, ALU.mult))
            link(tt_(dz[:, 9], li, li, ALU.mult))
            link(tt_(dz[:, 8], dz[:, 8], dz[:, 9], ALU.add))
            link(dve.reciprocal(dz[:, 9], dz[:, 8]))
            dve.wait_ge(sem("polar"), 3)
            p1r, p1i = dz[:, 10], dz[:, 11]
            link(tt_(p1r, dz[:, 2], dz[:, 4], ALU.mult))
            link(tt_(p1i, dz[:, 2], dz[:, 3], ALU.mult))
            link(ts_(dz[:, 12], p1r, -1.0, None, ALU.add))
            link(tt_(dz[:, 5], dz[:, 12], lr, ALU.mult))
            link(tt_(dz[:, 6], p1i, li, ALU.mult))
            link(tt_(dz[:, 5], dz[:, 5], dz[:, 6], ALU.add))
            link(tt_(cf[:, 0], dz[:, 5], dz[:, 9], ALU.mult))
            link(tt_(dz[:, 5], p1i, lr, ALU.mult))
            link(tt_(dz[:, 6], dz[:, 12], li, ALU.mult))
            link(tt_(dz[:, 5], dz[:, 5], dz[:, 6], ALU.subtract))
            link(tt_(cf[:, 1], dz[:, 5], dz[:, 9], ALU.mult))

            def powers(table, br_, bi_, n, past):
                view_ = lambda v: v.rearrange("p (l d q) -> p l d q", l=L, d=2)
                link(dve.memset(pc[:, 0], 1.0))
                link(dve.memset(pc[:, 1], 0.0))
                for p in range(n + 1):
                    cur, nxt = 2 * (p % 2), 2 * ((p + 1) % 2)
                    if p < n:
                        for r in range(2):
                            for d in range(2):
                                dve_ = dve.tensor_copy(table[:, r, :, d, :, p if d == 0 else n - 1 - p],
                                                       view_(pc[:, cur + r])[:, :, d])
                                link(dve_)
                    elif past is not None:
                        link(dve.tensor_copy(past[:], pc[:, cur:cur + 2]))
                    if p < n and (p < n - 1 or past is not None):
                        link(tt_(pc[:, nxt], pc[:, cur], br_, ALU.mult))
                        link(tt_(dz[:, 5], pc[:, cur + 1], bi_, ALU.mult))
                        link(tt_(pc[:, nxt], pc[:, nxt], dz[:, 5], ALU.subtract))
                        link(tt_(pc[:, nxt + 1], pc[:, cur], bi_, ALU.mult))
                        link(tt_(dz[:, 5], pc[:, cur + 1], br_, ALU.mult))
                        link(tt_(pc[:, nxt + 1], pc[:, nxt + 1], dz[:, 5], ALU.add))

            powers(pw, p1r, p1i, CL + 1, None)
            link(dve.tensor_copy(a1[:], pc[:, 0:2]))
            powers(aw, a1[:, 0], a1[:, 1], NB, a8)
            for s_, t_ in ((a1, a1s), (a8, a8s)):
                link(ts_(t_[:, 0], s_[:, 1], -1.0, None, ALU.mult))
                link(dve.tensor_copy(t_[:, 1], s_[:, 1]))

            def load_tables(l):
                dve.wait_ge(sem("bc_in"), 16 * 40 * (l + 1))
                b = [Braw[:, r].rearrange("p d (q h) -> p (d q) h", h=GH) for r in range(2)]
                o = [Bb[:, r].rearrange("p d q h -> p (d q) h") for r in range(2)]
                t = sg[:, 0, :].rearrange("p (x h) -> p x h", h=GH)
                k = [cf[:, r, 32 * l:32 * l + 32].rearrange("p (x h) -> p x h", h=1).broadcast_to([P, 32, GH]) for r in range(2)]
                link(tt_(o[0], b[0], k[0], ALU.mult))
                link(tt_(t, b[1], k[1], ALU.mult))
                link(tt_(o[0], o[0], t, ALU.subtract))
                link(tt_(o[1], b[1], k[0], ALU.mult))
                link(tt_(t, b[0], k[1], ALU.mult))
                tt_(o[1], o[1], t, ALU.add).then_inc(sem("bb_ready"), 1)
                dve.wait_ge(sem("bb_ready"), l + 1)
                for r in range(2):
                    dve.wait_ge(sem("c_turned"), 2 * l + r + 1)
                    dve.tensor_copy(Ct[:, r].rearrange("p d q h -> p (d q h)"), ps[:, r, :]).then_inc(sem("c_copied"), 1)
                dve.wait_ge(sem("c_copied"), 2 * l + 2)

            def cmul(o, u, v, n):
                t = sg[:].rearrange("p i t -> p (i t)")[:, 0:n].rearrange("p (q s h) -> p q s h", s=o[0].shape[2], h=GH)
                link(tt_(o[0], u[0], v[0], ALU.mult))
                link(tt_(t, u[1], v[1], ALU.mult))
                link(tt_(o[0], o[0], t, ALU.subtract))
                link(tt_(o[1], u[0], v[1], ALU.mult))
                link(tt_(t, u[1], v[0], ALU.mult))
                link(tt_(o[1], o[1], t, ALU.add))

            def prep(l, h):
                for qq in range(2):
                    n = 4 * l + 2 * h + qq
                    if qq == 0 and 2 * l + h:
                        dve.wait_ge(sem("y_chunks"), 4 * (2 * l + h))
                    if qq == 0:
                        for d in range(2):
                            for q0 in range(0, HQ, 4):
                                qs = slice(HQ * h + q0, HQ * h + q0 + 4)
                                o = [E[:, d, r, q0:q0 + 4].rearrange("p q (s h) -> p q s h", h=GH) for r in range(2)]
                                u = [Ct[:, r, d, qs].rearrange("p q (s h) -> p q s h", s=1).broadcast_to([P, 4, CL + 1, GH])
                                     for r in range(2)]
                                v = [pw[:, r, l, d, qs].rearrange("p q (s h) -> p q s h", h=1).broadcast_to([P, 4, CL + 1, GH])
                                     for r in range(2)]
                                cmul(o, u, v, 4 * (CL + 1) * GH)
                            link(ts_(E[:, d, 1], E[:, d, 1], -1.0, None, ALU.mult))
                    if n:
                        dve.wait_ge(sem("w_turned"), 4 * n)
                    for d in range(2):
                        qs = slice(HQ * h + 4 * qq, HQ * h + 4 * qq + 4)
                        o = [Fq[:, d, r].rearrange("p q (s h) -> p q s h", h=GH) for r in range(2)]
                        u = [Bb[:, r, d, qs].rearrange("p q (s h) -> p q s h", s=1).broadcast_to([P, 4, CL, GH]) for r in range(2)]
                        back = slice(CL - 1, None, -1) if d == 0 else slice(CL, 0, -1)
                        v = [pw[:, r, l, d, qs, back].rearrange("p q (s h) -> p q s h", h=1).broadcast_to([P, 4, CL, GH])
                             for r in range(2)]
                        cmul(o, u, v, 4 * CL * GH)
                    ts_(tick[:], eps_t[:], 0.0, None, ALU.mult).then_inc(sem("f_ready"), 1)
                    if n:
                        dve.wait_ge(sem("k_in"), 16 * 15 * n)
                    if qq == 0 and 2 * l + h:
                        dve.wait_ge(sem("z_turned"), 2 * (2 * l + h))
                    for i in range(4):
                        dve.wait_ge(sem("r_done"), 4 * n + i + 1)
                        dve.tensor_copy(R[:, i // 2, i % 2], ps[:, 4 + i, :].rearrange("p (q x) -> p q x", q=4))\
                            .then_inc(sem("r_copied"), 1)
                    dve.wait_ge(sem("r_copied"), 4 * n + 4)
                    diag = R[:, 0, :, :, 0:GH]
                    link(tt_(diag, diag, R[:, 1, :, :, P - GH:P], ALU.add))
                    t = sg[:, 0, 0:P].rearrange("p (a q h) -> p a q h", a=2, h=GH)
                    g0 = 2 * (HQ * h + 4 * qq)
                    dd = dT[:, l, g0:g0 + 8].rearrange("p (q a h) -> p a q h", a=2, h=1).broadcast_to([P, 2, 4, GH])
                    ey = eyeh[:].rearrange("p (a q h) -> p a q h", a=1, q=1).broadcast_to([P, 2, 4, GH])
                    link(tt_(t, ey, dd, ALU.mult))
                    tt_(diag, diag, t, ALU.add).then_inc(sem("r_ready"), 1)

            load_tables(0)
            prep(0, 0)

            dve.wait_ge(sem("step_used"), N_ADA)
            tt_(modT[:].rearrange("p l m s -> p (l m) s"), ps[:, 7, 0:2 * L * NM].rearrange("p (m s) -> p m s", s=2),
                bT[:].rearrange("p (m s) -> p m s", s=1).broadcast_to([P, L * NM, 2]), ALU.add).then_inc(sem("mod"), 1)
            dve.wait_ge(sem("mod"), 1)
            for l in range(L):
                for i, (g0, m0, one) in enumerate(((0, 1, 1.0), (16, 2, 0.0), (32, 4, 1.0), (48, 5, 0.0))):
                    gain = vT[:, g0 + KC * l:g0 + KC * l + KC].rearrange("p (k s) -> p k s", s=1).broadcast_to([P, KC, 2])
                    link(stt(amp[:, l, i], modT[:, l, KC * m0:KC * m0 + KC, :], one, gain, ALU.add, ALU.mult))

            def norm(n):
                cs = norm_cols(n)
                dve.wait_ge(sem("std_ready"), n + 1)
                link(dve.reciprocal(rstd[:, cs], std[:, cs]))

            def scale(n):
                norm(n)
                for k in range(KC):
                    for s, cs in streams(norm_cols(n)):
                        stt(aT[:, k, cs], hT[:, k, cs], amp[:, n // 4, n % 4, k, s:s + 1], rstd[:, cs], ALU.mult, ALU.mult)\
                            .then_inc(sem(f"scaled{n}"), 1)

            def add_back(n, y):
                norm(n)
                ss = streams(norm_cols(n))
                for k in range(KC):
                    for s, cs in ss:
                        stt(y(k, cs), y(k, cs), amp[:, n // 4, n % 4, k, s:s + 1], rstd[:, cs], ALU.mult, ALU.mult)\
                            .then_inc(sem(f"y_scaled{n}"), 1)
                    if k:
                        dve.wait_ge(sem(f"y_scaled{n}"), len(ss) * k)
                        cs = norm_cols(n)
                        tt_(hT[:, k - 1, cs], hT[:, k - 1, cs], y(k - 1, cs), ALU.add).then_inc(sem(f"h_ready{n}"), 1)
                dve.wait_ge(sem(f"y_scaled{n}"), len(ss) * KC)
                cs = norm_cols(n)
                tt_(hT[:, KC - 1, cs], hT[:, KC - 1, cs], y(KC - 1, cs), ALU.add).then_inc(sem(f"h_ready{n}"), 1)

            def copy_y(n, y):
                for m in range(KC):
                    dve.wait_ge(sem(f"y_done{n}"), m + 1)
                    dve.tensor_copy(y(m, norm_cols(n)), ps[:, m % 4, norm_cols(n)]).then_inc(sem(f"y_copied{n}"), 1)

            def recur(l, h):
                qs = slice(HQ * h, HQ * h + HQ)

                def coef(table, d):
                    v = table[:].rearrange("p r (l d q) -> p r l d q", l=L, d=2)
                    return v[:, :, l, d, qs]

                def fma(o, prev, c1, c2, nj, d):
                    w = HQ * nj
                    t = [tS[:, d, i, :, 0:w].rearrange("p r (q j) -> p r q j", j=nj) for i in range(2)]
                    shape = [P, 2, HQ, nj]
                    re = c1[:, 0:1].rearrange("p r (q j) -> p r q j", j=1).broadcast_to(shape)
                    im = c2.rearrange("p r (q j) -> p r q j", j=1).broadcast_to(shape)
                    flip = prev[:, ::-1]
                    yield tt_(t[0], prev, re, ALU.mult)
                    yield tt_(t[1], flip, im, ALU.mult)
                    yield tt_(o, o, t[0], ALU.add)
                    yield tt_(o, o, t[1], ALU.add)

                Xv = [X[:, d].rearrange("p r q (b i) -> p r q b i", i=NB) for d in range(2)]
                for s in range(1, NB):
                    pair = []
                    for d in range(2):
                        i, j = (s, s - 1) if d == 0 else (NB - 1 - s, NB - s)
                        pair.append(fma(Xv[d][:, :, :, :, i], Xv[d][:, :, :, :, j], coef(a1, d), coef(a1s, d), NB, d))
                    for ins in zip(*pair):
                        ins[0].then_inc(sem("scan"), 1)
                        link(ins[1])
                for d in range(2):
                    link(dve.tensor_copy(gcar[:, d].rearrange("p r q b -> p (r q) b"),
                                         Xv[d][:, :, :, :, NB - 1 if d == 0 else 0].rearrange("p r q b -> p (r q) b")))
                order = (list(range(NB)), [3, 2, 1, 0, 7, 6, 5, 4])
                for s in range(1, NB):
                    pair = []
                    for d in range(2):
                        i, j = order[d][s], order[d][s - 1]
                        pair.append(fma(gcar[:, d, :, :, i:i + 1], gcar[:, d, :, :, j:j + 1], coef(a8, d), coef(a8s, d), 1, d))
                    for ins in zip(*pair):
                        ins[0].then_inc(sem("scan"), 1)
                        link(ins[1])
                flat = lambda v: v.rearrange("p r q b -> p (r q) b")
                link(dve.memset(gpre, 0.0))
                link(dve.tensor_copy(flat(gpre[:, 0])[:, :, 1:8], flat(gcar[:, 0])[:, :, 0:7]))
                link(dve.tensor_copy(flat(gpre[:, 1])[:, :, 0:3], flat(gcar[:, 1])[:, :, 1:4]))
                link(dve.tensor_copy(flat(gpre[:, 1])[:, :, 4:7], flat(gcar[:, 1])[:, :, 5:8]))
                link(dve.tensor_copy(flat(gpre[:, 1])[:, :, 7:8], flat(gcar[:, 1])[:, :, 0:1]))
                for d in range(2):
                    for r in range(2):
                        t = [sg[:, i, :].rearrange("p (q b i) -> p q b i", q=HQ, b=NB) for i in range(2)]
                        shape = [P, HQ, NB, NB]
                        for i in range(2):
                            g = gpre[:, d, r if i == 0 else 1 - r].rearrange("p q (b i) -> p q b i", i=1).broadcast_to(shape)
                            k = aw[:, i, l, d, qs].rearrange("p q (b i) -> p q b i", b=1).broadcast_to(shape)
                            link(tt_(t[i], g, k, ALU.mult))
                        o = Pst[:, d, r].rearrange("p q (b i) -> p q b i", b=NB)
                        link(tt_(o, t[0], t[1], ALU.subtract if r == 0 else ALU.add))
                        ov = Pst[:, d, r].rearrange("p q (b i) -> p (q b) i", b=NB)
                        xv = X[:, d, r].rearrange("p q (b i) -> p (q b) i", b=NB)
                        to, fr = (slice(1, NB), slice(0, NB - 1)) if d == 0 else (slice(0, NB - 1), slice(1, NB))
                        link(tt_(ov[:, :, to], ov[:, :, to], xv[:, :, fr], ALU.add))
                ts_(tick[:], eps_t[:], 0.0, None, ALU.mult).then_inc(sem("p_ready"), 1)

            for l in range(L):
                lat = LAT if l else ALL
                n0 = 4 * l
                scale(n0)
                for m in range(MC):
                    dve.wait_ge(sem(f"vg_sig{l}"), m + 1)
                    st = slice(1, 2) if l else slice(0, 2)
                    tt_(apad[:, m, st, PAD:PAD + S], ps[:, 4 + 2 * (m % 2), lat].rearrange("p (i t) -> p i t", t=S),
                        sg[:, m % 2, lat].rearrange("p (i t) -> p i t", t=S), ALU.mult).then_inc(sem(f"gated{l}"), 1)
                if l:
                    load_tables(1)
                    prep(1, 0)
                for i in range(8):
                    dve.wait_ge(sem(f"u_turned{l}"), i + 1)
                    src = ps[0:HP, i % 4, :].rearrange("p (g j b) -> p b g j", g=4, b=2)
                    dve.tensor_copy(U[0:HP, 4 * i:4 * i + 4, :], src[:, 0])
                    dve.tensor_copy(U[HP:P, 4 * i:4 * i + 4, :], src[:, 1]).then_inc(sem(f"u_copied{l}"), 1)
                for h in range(2):
                    if h:
                        prep(l, 1)
                    dve.wait_ge(sem("x_states"), 4 * (2 * l + h + 1))
                    recur(l, h)
                for m in range(MC):
                    dve.wait_ge(sem(f"glu_sig{l}"), m + 1)
                    tt_(GO[:, m, lat], aT[:, m, lat], sg[:, m % 2, lat], ALU.mult).then_inc(sem(f"glu_used{l}"), 1)
                dve.wait_ge(sem(f"glu_used{l}"), MC)
                ts_(tick[:], eps_t[:], 0.0, None, ALU.mult).then_inc(sem(f"go_ready{l}"), MC)
                dve.wait_ge(sem(f"ln_sum{l}"), 1)
                link(ts_(rstd[:, lat], ps[:, 5, lat], 1.0 / DS, None, ALU.mult))
                for m in range(MC):
                    tt_(aT[:, MC + m, lat], aT[:, MC + m, lat], rstd[:, lat], ALU.subtract).then_inc(sem(f"centred{l}"), 1)
                dve.wait_ge(sem(f"ln_std{l}"), 1)
                dve.wait_ge(sem(f"centred{l}"), MC)
                link(dve.reciprocal(rstd[:, lat], std[:, lat]))
                for m in range(MC):
                    tt_(aT[:, MC + m, lat], aT[:, MC + m, lat], rstd[:, lat], ALU.mult).then_inc(sem(f"ln_scaled{l}"), 1)
                copy_y(n0 + 1, lambda k, cs: yE[:, k, cs])
                add_back(n0 + 1, lambda k, cs: yE[:, k, cs])
                dve.wait_ge(sem(f"h_ready{n0 + 1}"), KC)
                scale(n0 + 2)
                if l == 0:
                    for i in range(FN):
                        dve.wait_ge(sem("ffn_silu"), i + 1)
                        tt_(hid[:, i, :], sg[:, i % 2, :], ps[:, 2 * (i % 3) + 1, :], ALU.mult).then_inc(sem("hid_ready"), 1)
                    copy_y(3, lambda k, cs: aT[:, k, cs])
                    add_back(3, lambda k, cs: aT[:, k, cs])
                    dve.wait_ge(sem("h_ready3"), KC)

            dve.memset(acc, 0.0).then_inc(sem("acc_added"), 1)
            dve.wait_ge(sem("logits"), 1)
            link(dve.tensor_copy(lg[:], ps[:, 4, 0:2 * NE].rearrange("p (i e) -> p i e", i=2)))
            for i in range(2):
                link(dve.max(top[:, i], lg[:, i]))
                link(dve.max_index(topi[:, i], top[:, i], lg[:, i]))
            link(dve.tensor_copy(topf[:], topi[:]))
            for i in range(2):
                for j in range(2):
                    link(ts_(hot[:, i, j], iota_s[:, 0:NE], topf[:, i, j:j + 1], None, ALU.is_equal))
            tt_(gw[:, :, 0:1], top[:, :, 1:2], top[:, :, 0:1], ALU.subtract).then_inc(sem("top2"), 1)
            for i in range(2):
                tt_(mask[:, i], hot[:, i, 0], hot[:, i, 1], ALU.add).then_inc(sem("masked"), 1)
            dve.wait_ge(sem("gate_exp"), 1)
            link(ts_(gw[:, :, 2:3], gw[:, :, 1:2], 1.0, None, ALU.add))
            link(dve.reciprocal(gw[:, :, 3:4], gw[:, :, 2:3]))
            link(tt_(gw[:, :, 2:3], gw[:, :, 1:2], gw[:, :, 3:4], ALU.mult))
            for i in range(2):
                link(ts_(gate[:, i], hot[:, i, 0], gw[:, i, 3:4], None, ALU.mult))
                link(stt(gate[:, i], hot[:, i, 1], gw[:, i, 2:3], gate[:, i], ALU.mult, ALU.add))
            dve.wait_ge(sem("counted"), 1)
            dve.wait_ge(sem("masked"), 2)
            link(stt(slot_of[:], ps[:, 5, 0:2 * NE].rearrange("p (i e) -> p i e", i=2), UNROUTED, mask[:], ALU.add, ALU.mult))
            link(ts_(slot_of[:], slot_of[:], -UNROUTED, None, ALU.add))
            link(dve.tensor_reduce(most[:], ps[:, 5, 2 * NE:3 * NE], AX_X, ALU.max))
            dve.tensor_copy(most_i[:], most[:]).then_inc(sem("routed"), 1)

            def experts(ph):
                if ph:
                    ts_(slot_of[:], slot_of[:], -float(P), None, ALU.add).then_inc(sem("slots_down"), 1)
                    dve.wait_ge(sem("slots_down"), 1)
                for i in range(4):
                    dve.wait_ge(sem("ftok_turned"), 4 * ph + i + 1)
                    dve.tensor_copy(ftok[:, i // 2, 512 * (i % 2):512 * (i % 2) + 512], ps[:, i, :])\
                        .then_inc(sem("ftok_copied"), 1)
                for i in range(2):
                    for e in range(NE):
                        ts_(Sel[:, i, e, :], iota_s[:], slot_of[:, i, e:e + 1], None, ALU.is_equal).then_inc(sem("selected"), 1)
                        ts_(Sg[:, i, e, :], iota_s[:], slot_of[:, i, e:e + 1], gate[:, i, e:e + 1], ALU.is_equal, ALU.mult)\
                            .then_inc(sem("selected"), 1)
                with dve.Fori(0, NE) as e:
                    for c_ in range(NSTEP):
                        g = ph * NE * NSTEP + c_
                        dve.wait_ge(sem("sge_ready"), e * NSTEP + (g + 1))
                        if c_ >= 2:
                            dve.wait_ge(sem("dn_done"), e * NSTEP + (g - 1))
                        tt_(hide[:, c_ % 2], sge[:, c_ % 2, :].rearrange("p (f s) -> p f s", f=2),
                            ps[:, c_ % 2, 256:512].rearrange("p (f s) -> p f s", f=2), ALU.mult).then_inc(sem("hide_ready"), 1)
                    dve.wait_ge(sem("dn_done"), e * NSTEP + (ph * NE * NSTEP + NSTEP))
                    dve.tensor_copy(ysb[:, 512:1024], ps[:, 3, :]).then_inc(sem("ysb_ready"), 1)
                    for i in range(4):
                        dve.wait_ge(sem("spread"), e * 4 + (4 * NE * ph + i + 1))
                        a = acc[:, 2 * i:2 * i + 2, :].rearrange("p k t -> p (k t)")
                        tt_(a, a, ps[:, 4 + i, :], ALU.add).then_inc(sem("acc_added"), 1)
                dve.wait_ge(sem("acc_added"), 4 * NE * (ph + 1) + 1)

            dve.wait_ge(sem("acc_added"), 1)
            experts(0)
            dve.wait_ge(sem("routed"), 1)
            over = dve.value_load(most_i[0:1, 0:1], min_val=0, max_val=S)
            with dve.If(over > P):
                experts(1)
            ts_(tick[:], eps_t[:], 0.0, None, ALU.mult).then_inc(sem("summed"), 1)
            add_back(7, lambda k, cs: acc[:, k, :])
            for i in range(4):
                dve.wait_ge(sem("out_turned"), i + 1)
                ins = dve.tensor_copy(hT[:, 4 * (i // 2) + 2 * (i % 2):4 * (i // 2) + 2 * (i % 2) + 2, 0:S],
                                      ps[:, i, :].rearrange("p (k t) -> p k t", t=S))
                link(ins) if i % 2 == 0 else ins.then_inc(sem("rows_out"), 1)


_INS = ["x", "c", "ctx", "c_ctx", "w_ada", "b_ada", "g_pre_mix", "g_post_mix", "g_pre_ffn", "g_post_ffn", "w_in",
        "ssm_lam_re", "ssm_lam_im", "ssm_log_dt", "ssm_b_re", "ssm_b_im", "ssm_c_re", "ssm_c_im", "ssm_d",
        "ssm_w_glu", "ssm_b_glu", "conv_w", "conv_b", "conv_ln_g", "conv_ln_b", "w_out", "ffn_w_gate", "ffn_w_up",
        "ffn_w_down", "moe_w_router", "moe_b_router", "moe_w_gate", "moe_w_up", "moe_w_down"]
_OUTS = [((1, 256, 1024), "float32")]


def kernel(**inputs):
    import numpy as _np
    import concourse.bacc as _bacc
    from concourse import mybir as _mybir
    from concourse.bass_utils import run_bass_kernel_spmd as _run

    nc = _bacc.Bacc("TRN2", target_bir_lowering=False, num_devices=1)
    arrays, args = {}, []
    for name in _INS:
        a = _np.ascontiguousarray(inputs[name])
        arrays[f"in_{name}_dram"] = a
        args.append(nc.dram_tensor(f"in_{name}_dram", a.shape, _mybir.dt.from_np(a.dtype), kind="ExternalInput").ap())
    for i, (shape, dtype) in enumerate(_OUTS):
        dt = _mybir.dt.from_np(_np.dtype(dtype))
        args.append(nc.dram_tensor(f"out_{i}_dram", shape, dt, kind="ExternalOutput").ap())
    hybrid_backbone(nc, *args)
    r = _run(nc, [arrays], core_ids=[0])
    got = tuple(r.results[0][f"out_{i}_dram"] for i in range(len(_OUTS)))
    return got[0]
```

```python
from contextlib import ExitStack

import concourse.bass as bass
from concourse import mybir

ALU = mybir.AluOpType
ACT = mybir.ActivationFunctionType
AX_X = mybir.AxisListType.X
F32 = mybir.dt.float32
I32 = mybir.dt.int32
U32 = mybir.dt.uint32

P = 128
HP = 64
TWO_PI = 6.283185307179586
PI = 3.1415925
ROUND = 12582912.0
TWO_PI_HI = 6.28125
TWO_PI_MID = 0.0019350051879882812
TWO_PI_LO = 3.0199159819e-07
UNROUTED = 1024.0


def hybrid_backbone(nc, x, c, ctx_in, c_ctx, w_ada, b_ada, g_pre_mix, g_post_mix, g_pre_ffn, g_post_ffn, w_in,
                    lam_re, lam_im, log_dt, b_re, b_im, c_re, c_im, ssm_d, w_glu, b_glu, conv_w, conv_b,
                    ln_g, ln_b, w_out, ffn_gate, ffn_up, ffn_down, router_w, router_b, moe_gate, moe_up,
                    moe_down, out):
    _, S, D = x.shape
    T = 2 * S
    L = w_ada.shape[0]
    KC = D // P
    DS = ssm_d.shape[1]
    MC = DS // P
    G, NS, GH = b_re.shape[2:]
    Q = G // 2
    HQ = Q // 2
    CL = P // GH
    NJ = T // CL
    NB = 8
    CW = conv_w.shape[1]
    PAD = CW // 2
    FF = ffn_gate.shape[2]
    FN = FF // P
    NM = w_ada.shape[2] // P
    NE = router_w.shape[2]
    FE = moe_gate.shape[3]
    EPS = 1e-6
    LAT = slice(S, T)
    ALL = slice(0, T)
    assert (S, D, L, DS, G, NS, GH, FN) == (256, 1024, 2, 512, 32, 64, 16, 22) and FE == FF

    with ExitStack() as stack:
        sems = {}

        def sem(name):
            if name not in sems:
                sems[name] = stack.enter_context(nc.semaphore(name))
            return sems[name]

        def sb(name, shape, dt=F32):
            return stack.enter_context(nc.sbuf_tensor(name, shape, dt))

        hT = sb("hT", [P, KC, T])
        aT = sb("aT", [P, KC, T])
        SLOT = KC * 512
        ring = sb("ring", [P, 4 * SLOT])
        WORK = 18944
        work = sb("work", [P, WORK])
        apad = sb("apad", [P, MC, 2, S + 2 * PAD])
        ps = stack.enter_context(nc.psum_tensor("ps", [P, 8, 512], F32))

        def view(start, dims, names):
            size = 1
            for d in dims:
                size *= d
            return work[:, start:start + size].rearrange(f"p ({names}) -> p {names}", **dict(zip(names.split(), dims)))

        E = view(0, [2, 2, HQ, (CL + 1) * GH], "d r q x")
        Wst = view(4608, [2, 2, HQ, P], "d r q x")
        K = view(8704, [2, 2, 4, P], "f a q x")
        Fq = view(10752, [2, 2, 4, P], "d r q x")
        Pst = view(10752, [2, 2, HQ, NJ], "d r q j")
        R = view(12800, [2, 2, 4, P], "d a q x")
        yt = view(12800, [CL, 256], "t x")
        X = view(14848, [2, 2, HQ, NJ], "d r q j")
        T1 = view(14848, [G, 4, GH], "g i h")
        U = view(16896, [G, NJ], "g j")
        GO = view(16896, [MC, T], "m t")
        Braw = view(16896, [2, 2, Q * GH], "r d x")
        Craw = view(17920, [2, 4, P], "r d x")
        yE = view(0, [KC, T], "k t")
        rows_v = work[0:112, 12800:12928]
        rows_b = work[0:L * NM, 12928:13056]
        rows_z = work[0:64, 13056:13568].rearrange("p (k x) -> p k x", k=4)
        rows_w = work[0:L * CW, 13568:14080]
        rows_d = work[0:G, 14080:14336].rearrange("p (l s h) -> p l s h", l=L, s=CL)
        load_d = work[0:G, 14336:14368].rearrange("p (l h) -> p l h", l=L)
        load_dt = work[0:64, 14368:14370]
        dt = work[0:64, 14370:14372]
        zl = work[:, 4608:4864].rearrange("p (k x) -> p k x", k=4)
        dz = work[:, 4864:5760].rearrange("p (k x) -> p k x", k=14)
        hid = view(4608, [FN, T], "f t")
        xg = view(0, [NE, KC, P], "e k s")
        Gt = view(8192, [NE, S], "e t")
        acc = view(10240, [KC, S], "k t")
        ysb = view(12288, [D], "n")

        ident = sb("ident", [P, P])
        ones = sb("ones", [P, P])
        iota_s = sb("iota_s", [P, P])
        before = sb("before", [P, P])
        eyeh = sb("eyeh", [P, GH])
        eps_t = sb("eps_t", [P, 1])
        vT = sb("vT", [P, 112])
        bT = sb("bT", [P, L * NM])
        cwT = sb("cwT", [P, MC, L * CW])
        dT = sb("dT", [P, L, G])
        spare = ring[:, 3 * SLOT:4 * SLOT]
        pw = spare[:, 0:1152].rearrange("p (r l d q s) -> p r l d q s", r=2, l=L, d=2, q=Q)
        aw = sb("aw", [P, 2, L, 2, Q, NB])
        pc = sb("pc", [P, 4, 64])
        a1 = sb("a1", [P, 2, 64])
        a1s = sb("a1s", [P, 2, 64])
        a8 = sb("a8", [P, 2, 64])
        a8s = sb("a8s", [P, 2, 64])
        cf = sb("cf", [P, 2, 64])
        Bb = spare[:, 1152:2176].rearrange("p (r d q h) -> p r d q h", r=2, d=2, q=Q)
        Ct = spare[:, 2176:3200].rearrange("p (r d q h) -> p r d q h", r=2, d=2, q=Q)
        modT = sb("modT", [P, L, NM, 2])
        amp = sb("amp", [P, L, 4, KC, 2])
        sc = sb("sc", [P, KC, 2])
        sq = sb("sq", [P, 2, T])
        std = sb("std", [P, T])
        rstd = sb("rstd", [P, T])
        sg = sb("sg", [P, 2, T])
        mrow = [sq[0:2, 0, :], sq[0:2, 1, :], sg[0:2, 1, :]]
        gcar = std[:, 0:256].rearrange("p (b d r q) -> p b d r q", d=2, r=2, q=HQ)
        gpre = std[:, 256:512].rearrange("p (d r q b) -> p d r q b", d=2, r=2, q=HQ)
        tS = sg[:, 0, :].rearrange("p (d i r x) -> p d i r x", d=2, i=2, r=2)
        dg = sb("dg", [P, 4, P])
        wr = sb("wr", [P, KC, NE])
        br = sb("br", [1, NE])
        lg = sb("lg", [P, 2, NE])
        top = sb("top", [P, 2, 8])
        topi = sb("topi", [P, 2, 8], U32)
        topf = sb("topf", [P, 2, 8])
        hot = sb("hot", [P, 2, 2, NE])
        gw = sb("gw", [P, 2, 4])
        gate = sb("gate", [P, 2, NE])
        mask = sb("mask", [P, 2, NE])
        slot_of = sb("slot_of", [P, 2, NE])
        most = sb("most", [P, 1])
        most_i = sb("most_i", [P, 1], I32)
        tick = sb("tick", [P, 1])

        xin = aT[:, :, :].rearrange("p k t -> p (k t)").rearrange("p (i n) -> p i n", i=4)

        def slot(n):
            return ring[:, (n % 3) * SLOT:(n % 3 + 1) * SLOT]

        def cols(w, a, b, at=0):
            return at, w.shape[0] // P, b - a, w[:, a:b].rearrange("(k p) n -> p k n", p=P)

        ADA = NM // 4
        steps = [[cols(w_ada[l], 512 * i, 512 * i + 512)] for l in range(L) for i in range(ADA)]
        used = [("ada_done", n + 1) for n in range(len(steps))]
        N_ADA = len(steps)
        at = {}
        for l in range(L):
            at["in", l] = len(steps)
            steps += [[cols(w_in[l], 512 * i, 512 * i + 512)] for i in range(3)]
            used += [(f"u_done{l}", 4), (f"vg_done{l}", MC), (f"vg_done{l}", MC)]
            at["glu", l] = len(steps)
            steps += [[cols(w_glu[l], 0, DS)]]
            used += [(f"glu_done{l}", MC)]
            at["out", l] = len(steps)
            steps += [[cols(w_out[l], 512 * i, 512 * i + 512)] for i in range(2)]
            used += [(f"y_done{4 * l + 1}", 4 * i + 4) for i in range(2)]
            if l == 0:
                at["ffn"] = len(steps)
                steps += [[cols(ffn_gate[0], 256 * i, 256 * i + 256), cols(ffn_up[0], 256 * i, 256 * i + 256, 2048)]
                          for i in range(FN // 2)]
                used += [("ffn_done", 2 * i + 2) for i in range(FN // 2)]
                at["down"] = len(steps)
                steps += [[cols(ffn_down[0], P * i, P * i + P)] for i in range(KC)]
                used += [("y_done3", i + 1) for i in range(KC)]
        landed = []
        per_slot = [0, 0, 0]
        for n, s in enumerate(steps):
            per_slot[n % 3] += 16 * len(s)
            landed.append(per_slot[n % 3])

        def weights(n, i=0):
            a, k, w, _ = steps[n][i]
            return slot(n)[:, a:a + k * w].rearrange("p (k w) -> p k w", k=k)

        def norm_cols(n):
            return LAT if n > 4 else ALL

        def streams(cs):
            return [(1, LAT)] if cs == LAT else [(0, slice(0, S)), (1, LAT)]

        GU = [ring[:, 4096 * i:4096 * (i + 1)].rearrange("p (a k f) -> p a k f", a=2, k=KC) for i in range(4)]
        Sel = view(13312, [2, NE, P], "i e s")
        Sg = view(15360, [2, NE, P], "i e s")
        flat_pad = apad[:].rearrange("p m i t -> p (m i t)")[:, 0:2 * D]
        ftok = flat_pad.rearrange("p (i n) -> p i n", i=2)
        DN = [view(13312, [2, D], "f n"), view(15360, [2, D], "f n"), flat_pad.rearrange("p (f n) -> p f n", f=2)]
        hide = work[:, 17408:17920].rearrange("p (b f s) -> p b f s", b=2, f=2)
        sge = work[:, 17920:18432].rearrange("p (b n) -> p b n", b=2)
        NSTEP = FE // 256
        USES = [3, 3, 3, 2]
        DUSES = [4, 4, 3]

        block = stack.enter_context(nc.Block())

        @block.sync
        def _(sp):
            def load(n):
                if n >= 3:
                    name, count = used[n - 3]
                    sp.wait_ge(sem(name), count)
                for i, (_, _, _, src) in enumerate(steps[n]):
                    sp.dma_start(weights(n, i), src).then_inc(sem(f"ring_in{n % 3}"), 16)

            def load_bc(l):
                for i, w in enumerate((b_re, b_im)):
                    for d in range(2):
                        for a in range(2):
                            sp.dma_start(Braw[HP * a:HP * a + HP, i, d].rearrange("p (q h) -> p q h", h=GH),
                                          w[l, d].rearrange("(q a) p h -> a p q h", a=2)[a]).then_inc(sem("bc_in"), 16)
                for i, w in enumerate((c_re, c_im)):
                    for q in range(HQ):
                        src = w[l].rearrange("d (f q a) h p -> q a h (d f) p", f=2, a=2)[q]
                        for a in range(2):
                            sp.dma_start(Craw[GH * q:GH * q + GH, i, :, HP * a:HP * a + HP], src[a])\
                                .then_inc(sem("bc_in"), 16)

            for i, src in enumerate((ctx_in, x)):
                sp.dma_start(xin[:, 2 * i:2 * i + 2, :], src[0].rearrange("(i p) n -> p i n", p=P)).then_inc(sem("x_in"), 16)
            sp.wait_ge(sem("rows_in"), 16 * 16)
            for n in range(3):
                load(n)
            load_bc(0)
            for l in range(L):
                src = w_ada[l].rearrange("(k p) n -> p k n", p=P)
                with sp.Fori(1 if l == 0 else 0, ADA // 3) as it:
                    for s in range(3):
                        sp.wait_ge(sem("ada_done"), 3 * it + (l * ADA + s - 2))
                        sp.dma_start(weights(s), src[:, :, bass.ds(it * 1536 + 512 * s, 512)]).then_inc(sem(f"ring_in{s}"), 16)
            for n in range(N_ADA, len(steps)):
                load(n)
                if n == at["ffn"] + 2:
                    sp.wait_ge(sem("y_done1"), KC)
                    load_bc(1)

            def load_gu(e, c):
                for i, w in enumerate((moe_gate, moe_up)):
                    sp.dma_start(GU[c % 4][:, i], w[0, e, :, 256 * c:256 * c + 256].rearrange("(k p) n -> p k n", p=P))\
                        .then_inc(sem(f"gu_in{c % 4}"), 16)

            def load_dn(e, c):
                sp.dma_start(DN[c % 3], moe_down[0, e, 256 * c:256 * c + 256, :].rearrange("(f p) n -> p f n", p=P))\
                    .then_inc(sem(f"dn_in{c % 3}"), 16)

            def experts(ph):
                g0 = ph * NE * NSTEP
                if ph:
                    sp.wait_ge(sem("dn_done"), g0)
                else:
                    sp.wait_ge(sem("y_done5"), KC)
                for c in range(4):
                    load_gu(0, c)
                sp.wait_ge(sem("moved"), 20 * (ph + 1))
                for c in range(3):
                    load_dn(0, c)

                def body(e, last):
                    for c in range(NSTEP):
                        if c + 4 < NSTEP or not last:
                            after = c if c + 4 < NSTEP else (8, 9, 10, 7)[c + 4 - NSTEP]
                            sp.wait_ge(sem("gu_done"), e * NSTEP + (g0 + after + 1))
                            load_gu(e if c + 4 < NSTEP else e + 1, (c + 4) % NSTEP)
                        if c >= 1 and (c + 2 < NSTEP or not last):
                            after = c - 1 if c + 2 < NSTEP else (9, 10)[c + 2 - NSTEP]
                            sp.wait_ge(sem("dn_done"), e * NSTEP + (g0 + after + 1))
                            load_dn(e if c + 2 < NSTEP else e + 1, (c + 2) % NSTEP)
                    if not last:
                        load_dn(e + 1, 2)

                with sp.Fori(0, NE - 1) as e:
                    body(e, False)
                body(NE - 1, True)

            experts(0)
            sp.wait_ge(sem("routed"), 1)
            over = sp.value_load(most_i[0:1, 0:1], min_val=0, max_val=S)
            with sp.If(over > P):
                experts(1)
            sp.wait_ge(sem("rows_out"), 2)
            for i in range(2):
                sp.dma_start(out[0, i * P:(i + 1) * P, :], hT[:, 4 * i:4 * i + 4, 0:S]).then_inc(sem("out_done"), 16)
            sp.wait_ge(sem("out_done"), 32)

        @block.gpsimd
        def _(pool):
            n = sem("consts")
            pool.memset(ident[:], 0.0).then_inc(n, 1)
            pool.memset(ones[:], 1.0).then_inc(n, 1)
            pool.memset(eps_t[:], EPS).then_inc(n, 1)
            pool.memset(apad[:], 0.0).then_inc(n, 1)
            pool.iota(iota_s[:], pattern=[[1, P]], base=0, channel_multiplier=0,
                      allow_small_or_imprecise_dtypes=True).then_inc(n, 1)
            pool.wait_ge(n, 5)
            pool.affine_select(out=ident[:], in_=ident[:], compare_op=ALU.not_equal, fill=1.0, base=0,
                               pattern=[[-1, P]], channel_multiplier=1).then_inc(n, 1)
            pool.affine_select(out=before[:], in_=ones[:], compare_op=ALU.is_gt, fill=0.0, base=0,
                               pattern=[[1, P]], channel_multiplier=-1).then_inc(n, 1)
            pool.wait_ge(n, 7)
            pool.wait_ge(sem("par"), 5)
            i = 0
            for l in range(L):
                for m in range(MC):
                    for k in range(CW):
                        if i >= 4:
                            pool.wait_ge(sem("tap_used"), i - 3)
                        pool.tensor_scalar(dg[:, i % 4, :], ident[:], cwT[:, m, l * CW + k:l * CW + k + 1], 0.0,
                                           ALU.mult, ALU.add).then_inc(sem("tap"), 1)
                        i += 1

        @block.scalar
        def _(act):
            r = sem("rows_in")
            row = 0
            for w in (g_pre_mix, g_post_mix, g_pre_ffn, g_post_ffn, b_glu, conv_b, ln_g, ln_b):
                k = L * w.shape[1] // P
                act.dma_start(rows_v[row:row + k], w.rearrange("l (c p) -> (l c) p", p=P)).then_inc(r, 16)
                row += k
            act.dma_start(rows_v[row:row + KC], c_ctx.rearrange("(c p) -> c p", p=P)).then_inc(r, 16)
            act.dma_start(rows_v[row + KC:row + 2 * KC], c[0].rearrange("(c p) -> c p", p=P)).then_inc(r, 16)
            act.dma_start(rows_b, b_ada.rearrange("l (c p) -> (l c) p", p=P)).then_inc(r, 16)
            act.dma_start(rows_w, conv_w.rearrange("l k n -> (l k) n")).then_inc(r, 16)
            act.dma_start(rows_z[:, 2], lam_re.rearrange("l d (q a) p -> (l d q) (a p)", a=2)).then_inc(r, 16)
            act.dma_start(rows_z[:, 3], lam_im.rearrange("l d (q a) p -> (l d q) (a p)", a=2)).then_inc(r, 16)
            act.dma_start(load_dt, log_dt.rearrange("l d (q a) -> (l d q) a", a=2)).then_inc(r, 16)
            act.dma_start(load_d, ssm_d.rearrange("l (g h) -> g l h", h=GH)).then_inc(r, 16)

            act.dma_start(wr[:], router_w[0].rearrange("(k p) e -> p k e", p=P)).then_inc(sem("router_in"), 16)
            act.dma_start(br[:], router_b).then_inc(sem("router_in"), 16)
            act.wait_ge(r, 16 * 16)
            act.activation(dt, load_dt, ACT.Exp).then_inc(sem("dt"), 1)

            act.wait_ge(sem("par"), 5)
            act.activation(sc[:].rearrange("p k s -> p s k"), vT[:, 96:112].rearrange("p (s k) -> p s k", s=2),
                           ACT.Silu).then_inc(sem("silu_c"), 1)
            for k in range(KC):
                act.wait_ge(sem("x_turned"), k + 1)
                act.activation(hT[:, k, :], ps[:, 3 + k % 4, :], ACT.Copy).then_inc(sem("x_copied"), 1)
            act.wait_ge(sem("angle"), 1)
            act.activation(dz[:, 2], zl[:, 0], ACT.Exp).then_inc(sem("polar"), 1)
            act.activation(dz[:, 3], dz[:, 0], ACT.Sin).then_inc(sem("polar"), 1)
            act.activation(dz[:, 4], dz[:, 1], ACT.Sin).then_inc(sem("polar"), 1)
            def prep(l, h, qq):
                n = 4 * l + 2 * h + qq
                for i in range(4):
                    act.wait_ge(sem("w_turned"), 4 * n + i + 1)
                    act.activation(Wst[:, i // 2, i % 2, 4 * qq:4 * qq + 4, :],
                                   ps[:, i, :].rearrange("p (q x) -> p q x", q=4), ACT.Copy).then_inc(sem("w_copied"), 1)
                for i in range(4):
                    d, r_ = i // 2, i % 2
                    b = Bb[:, r_, d, HQ * h + 4 * qq:HQ * h + 4 * qq + 4, :].rearrange("p q (s h) -> p q s h", s=1)
                    act.activation(Fq[:, d, r_].rearrange("p q (s h) -> p q s h", h=GH), b.broadcast_to([P, 4, CL, GH]),
                                   ACT.Copy).then_inc(sem("b_spread"), 1)
                act.wait_ge(sem("r_ready"), n + 1)
                if 2 * l + h:
                    act.wait_ge(sem("y_chunks"), 4 * (2 * l + h))
                for s in range(CL):
                    row = slice(GH * s, GH * s + GH)
                    act.dma_start(K[row, qq, :, :, GH * s:P].rearrange("p a q x -> p (a q) x"),
                                  R[row, 0, :, :, 0:P - GH * s].rearrange("p a q x -> p (a q) x")).then_inc(sem("k_in"), 16)
                    if s:
                        act.dma_start(K[row, qq, :, :, 0:GH * s].rearrange("p a q x -> p (a q) x"),
                                      R[row, 1, :, :, P - GH - GH * s:P - GH].rearrange("p a q x -> p (a q) x")).then_inc(sem("k_in"), 16)

            def norm(n, src, ready):
                cs = norm_cols(n)
                for k in range(KC):
                    i = KC * n + k
                    ready(k)
                    if i >= 2:
                        act.wait_ge(sem("sq_used"), i - 1)
                    act.activation(sq[:, i % 2, cs], src(k), ACT.Square).then_inc(sem("sq_ready"), 1)
                act.wait_ge(sem("sq_used"), KC * n + KC)
                act.activation(std[:, cs], ps[:, 6, cs], ACT.Sqrt, bias=eps_t[:, 0:1], scale=1.0 / D)\
                    .then_inc(sem("std_ready"), 1)

            def shift(n):
                l, i = n // 4, 3 * (n % 4 // 2)
                for k in range(KC):
                    for j, (s, cols_) in enumerate(streams(norm_cols(n))):
                        act.wait_ge(sem(f"scaled{n}"), k * len(streams(norm_cols(n))) + j + 1)
                        act.activation(aT[:, k, cols_], aT[:, k, cols_], ACT.Identity,
                                       bias=modT[:, l, KC * i + k, s:s + 1]).then_inc(sem(f"a_ready{n}"), 1)

            def conv_out(l, m):
                cs = LAT if l else ALL
                act.wait_ge(sem(f"conv_done{l}"), m + 1)
                act.activation(aT[:, MC + m, cs], ps[:, 6 if m == 3 else 7, cs], ACT.Identity,
                               bias=vT[:, 72 + MC * l + m:73 + MC * l + m]).then_inc(sem(f"conv_copied{l}"), 1)

            norm(0, lambda k: hT[:, k, :], lambda k: act.wait_ge(sem("x_copied"), k + 1))
            with act.Fori(0, N_ADA // 3) as it:
                for s in range(3):
                    act.wait_ge(sem("ada_done"), it * 3 + (s + 1))
                    act.activation(mrow[s], ps[0:2, s, :], ACT.Copy).then_inc(sem("mod_row"), 1)
            act.wait_ge(sem("mod_turned"), N_ADA)
            for l in range(L):
                lat = LAT if l else ALL
                n0 = 4 * l
                if l:
                    norm(n0, lambda k: hT[:, k, norm_cols(n0)], lambda k: act.wait_ge(sem("h_ready3"), k + 1))
                shift(n0)
                for i in range(4):
                    act.wait_ge(sem(f"u_done{l}"), i + 1)
                    act.activation(T1[:, :, i, :], ps[:, i, :].rearrange("p (g h) -> p g h", h=GH), ACT.Copy).then_inc(sem(f"t1_copied{l}"), 1)
                prep(l, 0, 0)
                for m in range(MC):
                    act.wait_ge(sem(f"vg_done{l}"), m + 1)
                    if m >= 2:
                        act.wait_ge(sem(f"gated{l}"), m - 1)
                    act.activation(sg[:, m % 2, lat], ps[:, 5 + 2 * (m % 2), lat], ACT.Sigmoid).then_inc(sem(f"vg_sig{l}"), 1)
                prep(l, 0, 1)
                for h in range(2):
                    if h:
                        for qq in range(2):
                            prep(l, 1, qq)
                    for i in range(4):
                        act.wait_ge(sem("x_done"), 4 * (2 * l + h) + i + 1)
                        act.activation(X[:, i // 2, i % 2], ps[:, i, :].rearrange("p (q j) -> p q j", q=HQ), ACT.Copy)\
                            .then_inc(sem("x_states"), 1)
                    for m in ((2, 3) if h else (0,)):
                        conv_out(l, m)
                    for i in range(4):
                        act.wait_ge(sem("y_chunks"), 4 * (2 * l + h) + i + 1)
                        g2, b = i // 2, i % 2
                        dst = yt[0:NJ].rearrange("p t (q a h) -> p a q t h", a=2, h=GH)[:, g2, 4 * b:4 * b + 4]
                        act.activation(dst, ps[0:NJ, i, :].rearrange("p (q t h) -> p q t h", q=4, h=GH), ACT.Copy)\
                            .then_inc(sem("yt_copied"), 1)
                    for i in range(2):
                        act.wait_ge(sem("z_turned"), 2 * (2 * l + h) + i + 1)
                        act.activation(aT[:, 2 * h + i, :].rearrange("p (j t) -> p j t", t=CL),
                                       ps[:, 4 + i, :].rearrange("p (t j) -> p j t", t=CL), ACT.Gelu_apprx_tanh)\
                            .then_inc(sem(f"z_ready{l}"), 1)
                    if h == 0:
                        conv_out(l, 1)
                for m in range(MC):
                    act.wait_ge(sem(f"glu_done{l}"), m + 1)
                    if m >= 2:
                        act.wait_ge(sem(f"glu_used{l}"), m - 1)
                    act.activation(sg[:, m % 2, lat], ps[:, m, lat], ACT.Sigmoid,
                                   bias=vT[:, 64 + MC * l + m:65 + MC * l + m]).then_inc(sem(f"glu_sig{l}"), 1)
                for m in range(MC):
                    act.wait_ge(sem(f"centred{l}"), m + 1)
                    if m >= 2:
                        act.wait_ge(sem(f"ln_used{l}"), m - 1)
                    act.activation(sq[:, m % 2, lat], aT[:, MC + m, lat], ACT.Square).then_inc(sem(f"ln_sq{l}"), 1)
                act.wait_ge(sem(f"ln_used{l}"), MC)
                act.activation(std[:, lat], ps[:, 6, lat], ACT.Sqrt, bias=eps_t[:, 0:1], scale=1.0 / DS)\
                    .then_inc(sem(f"ln_std{l}"), 1)
                for m in range(MC):
                    act.wait_ge(sem(f"ln_scaled{l}"), m + 1)
                    act.activation(aT[:, MC + m, lat], aT[:, MC + m, lat], ACT.Silu,
                                   scale=vT[:, 80 + MC * l + m:81 + MC * l + m],
                                   bias=vT[:, 88 + MC * l + m:89 + MC * l + m]).then_inc(sem(f"cv_ready{l}"), 1)
                norm(n0 + 1, lambda k: yE[:, k, lat], lambda k: act.wait_ge(sem(f"y_copied{n0 + 1}"), k + 1))
                norm(n0 + 2, lambda k: hT[:, k, lat], lambda k: act.wait_ge(sem(f"h_ready{n0 + 1}"), k + 1))
                shift(n0 + 2)
                if l == 0:
                    for i in range(FN):
                        act.wait_ge(sem("ffn_done"), i + 1)
                        if i >= 2:
                            act.wait_ge(sem("hid_ready"), i - 1)
                        act.activation(sg[:, i % 2, :], ps[:, 2 * (i % 3), :], ACT.Silu).then_inc(sem("ffn_silu"), 1)
                    norm(3, lambda k: aT[:, k, :], lambda k: act.wait_ge(sem("y_copied3"), k + 1))

            act.wait_ge(sem("top2"), 1)
            act.activation(gw[:, :, 1:2], gw[:, :, 0:1], ACT.Exp).then_inc(sem("gate_exp"), 1)

            def experts(ph):
                for i in range(16):
                    act.wait_ge(sem("gathered"), 16 * ph + i + 1)
                    act.activation(xg[:, 4 * (i % 2):4 * (i % 2) + 4, i // 2, :],
                                   ps[:, i % 4, :].rearrange("p (e s) -> p e s", e=4), ACT.Copy).then_inc(sem("moved"), 1)
                for i in range(4):
                    act.wait_ge(sem("gates_turned"), 4 * ph + i + 1)
                    act.activation(Gt[:, 4 * (i % 2):4 * (i % 2) + 4, P * (i // 2):P * (i // 2) + P],
                                   ps[:, 4 + i, :].rearrange("p (e s) -> p e s", e=4), ACT.Copy).then_inc(sem("moved"), 1)
                with act.Fori(0, NE) as e:
                    for c_ in range(NSTEP):
                        g = ph * NE * NSTEP + c_
                        act.wait_ge(sem("gu_done"), e * NSTEP + (g + 1))
                        if c_ >= 2:
                            act.wait_ge(sem("hide_ready"), e * NSTEP + (g - 1))
                        act.activation(sge[:, c_ % 2, :], ps[:, c_ % 2, 0:256], ACT.Silu).then_inc(sem("sge_ready"), 1)
                    act.wait_ge(sem("dn_done"), e * NSTEP + (ph * NE * NSTEP + NSTEP))
                    act.activation(ysb[:, 0:512], ps[:, 2, :], ACT.Copy).then_inc(sem("ysb_ready"), 1)

            experts(0)
            act.wait_ge(sem("routed"), 1)
            over = act.value_load(most_i[0:1, 0:1], min_val=0, max_val=S)
            with act.If(over > P):
                experts(1)
            norm(7, lambda k: acc[:, k, :], lambda k: act.wait_ge(sem("summed"), 1))

        @block.tensor
        def _(pe):
            def mm(o, lhs, rhs, start=True, stop=True):
                return pe.matmul(o, lhs, rhs, start=start, stop=stop)

            def turn(o, i, n=P):
                return pe.transpose(o, i, ident[0:n, 0:n])

            def step_in(n):
                pe.wait_ge(sem(f"ring_in{n % 3}"), landed[n])

            pe.wait_ge(sem("consts"), 7)
            pe.wait_ge(sem("rows_in"), 16 * 16)
            turn(ps[:, 0, 0:112], rows_v, 112)
            turn(ps[:, 0, 128:128 + L * NM], rows_b, L * NM)
            for m in range(MC):
                turn(ps[:, 1, L * CW * m:L * CW * (m + 1)], rows_w[:, P * m:P * m + P], L * CW)
            pe.wait_ge(sem("z_rows"), 5)
            for l in range(L):
                turn(ps[:, 1, 256 + G * l:256 + G * l + G], rows_d[:, l].rearrange("p s h -> p (s h)"), G)
            for i in range(4):
                last = turn(ps[:, 2, 64 * i:64 * i + 64], rows_z[:, i, :], 64)
            last.then_inc(sem("rows_turned"), 1)
            pe.wait_ge(sem("x_in"), 32)
            for k in range(KC):
                if k >= 4:
                    pe.wait_ge(sem("x_copied"), k - 3)
                for i in range(4):
                    last = turn(ps[:, 3 + k % 4, P * i:P * i + P], xin[:, i, P * k:P * k + P])
                last.then_inc(sem("x_turned"), 1)

            def turn_c(l):
                pe.wait_ge(sem("bc_in"), 16 * 40 * (l + 1))
                pe.wait_ge(sem("std_ready"), 2 * l + 1)
                for i in range(2):
                    for j in range(4):
                        last = turn(ps[:, 5 + l + i, P * j:P * j + P], Craw[:, i, j, :])
                    last.then_inc(sem("c_turned"), 1)

            def prep(l, h, qq):
                n = 4 * l + 2 * h + qq
                if h:
                    if qq == 0:
                        pe.wait_ge(sem(f"z_ready{l}"), 2)
                        pe.wait_ge(sem(f"conv_copied{l}"), 2)
                elif qq == 0:
                    pe.wait_ge(sem(f"t1_copied{l}"), 4)
                else:
                    pe.wait_ge(sem(f"u_copied{l}"), 8)
                    pe.wait_ge(sem(f"gated{l}"), MC)
                pe.wait_ge(sem("f_ready"), n + 1)
                if n:
                    pe.wait_ge(sem("w_copied"), 4 * n)
                if qq == 0 and h == 0:
                    pe.wait_ge(sem("c_copied"), 2 * (l + 1))
                for i in range(4):
                    for q in range(4):
                        last = turn(ps[:, i, P * q:P * q + P], Fq[:, i // 2, i % 2, q, :])
                    last.then_inc(sem("w_turned"), 1)
                if n:
                    pe.wait_ge(sem("r_copied"), 4 * n)
                pe.wait_ge(sem("b_spread"), 4 * (n + 1))
                pe.wait_ge(sem("out_table"), 2 * (2 * l + h + 1))
                for d in range(2):
                    for a in range(2):
                        rows = slice(HP * a, HP * a + HP)
                        for q in range(4):
                            for r in range(2):
                                last = mm(ps[:, 4 + 2 * d + a, P * q:P * q + P], Fq[rows, d, r, q, :],
                                          E[rows, d, r, 4 * qq + q, GH * d:GH * d + P], start=r == 0, stop=r == 1)
                        last.then_inc(sem("r_done"), 1)

            def norm(n):
                cs = norm_cols(n)
                for k in range(KC):
                    pe.wait_ge(sem("sq_ready"), KC * n + k + 1)
                    mm(ps[:, 6, cs], ones[:], sq[:, (KC * n + k) % 2, cs], k == 0, k == KC - 1).then_inc(sem("sq_used"), 1)

            pe.wait_ge(sem("x_copied"), KC)
            norm(0)
            pe.wait_ge(sem("silu_c"), 1)
            pe.wait_ge(sem("par"), 5)
            mod_ps = ps[:, 7, 0:2 * L * NM]

            def turn_mod(it, s):
                pe.wait_ge(sem("mod_row"), it * 3 + (s + 1))
                for m in range(4):
                    last = mm(mod_ps[:, bass.ds(it * 24 + (8 * s + 2 * m), 2)], mrow[s][:, P * m:P * m + P], ident[0:2, 0:2])
                last.then_inc(sem("mod_turned"), 1)

            def modulation(r0, r1):
                with pe.Fori(r0, r1) as it:
                    for s in range(3):
                        pe.wait_ge(sem(f"ring_in{s}"), it * 16 + 16)
                        w = weights(s)
                        for k in range(KC):
                            last = mm(ps[0:2, s, :], sc[:, k, :], w[:, k, :], k == 0, k == KC - 1)
                        last.then_inc(sem("ada_done"), 1)
                        if s:
                            turn_mod(it, s - 1)
                    turn_mod(it, 2)

            modulation(0, 2)
            turn_c(0)
            modulation(2, N_ADA // 3)
            pe.wait_ge(sem("mod"), 1)

            def conv(l, m):
                lat = slice(1, 2) if l else slice(0, 2)
                if m == 0:
                    pe.wait_ge(sem(f"gated{l}"), MC)
                if m % 2 == 0:
                    pe.wait_ge(sem("r_copied"), 8 * (2 * l + m // 2 + 1))
                if m in (1, 2):
                    pe.wait_ge(sem(f"conv_copied{l}"), m)
                o = ps[:, 6 if m == 3 else 7, LAT if l else ALL].rearrange("p (i t) -> p i t", t=S)
                for k in range(CW):
                    i = (l * MC + m) * CW + k
                    pe.wait_ge(sem("tap"), i + 1)
                    last = mm(o, dg[:, i % 4, :], apad[:, m, lat, k:k + S], k == 0, k == CW - 1)
                    last.then_inc(sem("tap_used"), 1)
                pe.wait_ge(sem("tap_used"), (l * MC + m + 1) * CW)
                pe.sem_inc(sem(f"conv_done{l}"), 1)

            def project(n, w_at, width, rhs, ready, nk, cs):
                for m in range(KC):
                    if m * P % width == 0:
                        step_in(w_at + m * P // width)
                    if m >= 4:
                        pe.wait_ge(sem(f"y_copied{n}"), m - 3)
                    w = weights(w_at + m * P // width)
                    for k in range(nk):
                        if m == 0:
                            ready(k)
                        last = mm(ps[:, m % 4, cs], w[:, k, m * P % width:m * P % width + P], rhs(k), k == 0, k == nk - 1)
                    last.then_inc(sem(f"y_done{n}"), 1)

            for l in range(L):
                lat = LAT if l else ALL
                n0 = 4 * l
                if l:
                    norm(n0)
                n_in = at["in", l]
                step_in(n_in)
                w = weights(n_in)
                for i in range(4):
                    for k in range(KC):
                        if i == 0:
                            pe.wait_ge(sem(f"a_ready{n0}"), 2 * k + 2)
                        last = mm(ps[:, i, :], aT[:, k, i:T:4], w[:, k, :], k == 0, k == KC - 1)
                    last.then_inc(sem(f"u_done{l}"), 1)
                prep(l, 0, 0)
                pe.wait_ge(sem("w_copied"), 16 * l + 4)
                for i in range(8):
                    if i >= 4:
                        pe.wait_ge(sem(f"u_copied{l}"), i - 3)
                    for g in range(4):
                        last = turn(ps[0:HP, i % 4, P * g:P * g + P], T1[:, 4 * i + g].rearrange("p i h -> p (i h)"))
                    last.then_inc(sem(f"u_turned{l}"), 1)
                pe.wait_ge(sem("r_copied"), 16 * l + 4)
                step_in(n_in + 1)
                step_in(n_in + 2)
                for m in range(MC):
                    if m >= 2:
                        pe.wait_ge(sem(f"gated{l}"), m - 1)
                    for i in range(2):
                        w = weights(n_in + 1 + i)
                        for k in range(KC):
                            last = mm(ps[:, 4 + i + 2 * (m % 2), lat], w[:, k, P * m:P * m + P], aT[:, k, lat], k == 0, k == KC - 1)
                    last.then_inc(sem(f"vg_done{l}"), 1)
                prep(l, 0, 1)
                for h in range(2):
                    hh = 2 * l + h
                    if h:
                        for qq in range(2):
                            prep(l, 1, qq)
                    pe.wait_ge(sem(f"u_copied{l}"), 8)
                    pe.wait_ge(sem("w_copied"), 8 * (hh + 1))
                    for i in range(4):
                        for q in range(HQ):
                            for a in range(2):
                                last = mm(ps[HP * a:HP * a + HP, i, NJ * q:NJ * q + NJ],
                                          Wst[:, i // 2, i % 2, q, HP * a:HP * a + HP], U[:, 2 * (HQ * h + q) + a, :])
                        last.then_inc(sem("x_done"), 1)
                    for m in ((2, 3) if h else (0,)):
                        conv(l, m)
                    pe.wait_ge(sem("k_in"), 16 * 15 * 2 * (hh + 1))
                    pe.wait_ge(sem("p_ready"), hh + 1)
                    for i in range(4):
                        a, b = i // 2, i % 2
                        rows = slice(HP * a, HP * a + HP)
                        for qi in range(4):
                            q = 4 * b + qi
                            o = ps[0:NJ, i, P * qi:P * qi + P]
                            mm(o, U[:, 2 * (HQ * h + q) + a, :], K[:, b, a, qi, :], True, False)
                            for d in range(2):
                                for r in range(2):
                                    lo = GH * (1 - d)
                                    last = mm(o, Pst[rows, d, r, q, :], E[rows, d, r, q, lo:lo + P], False, d == 1 and r == 1)
                        last.then_inc(sem("y_chunks"), 1)
                    pe.wait_ge(sem("yt_copied"), 4 * (hh + 1))
                    for i in range(2):
                        for t in range(CL):
                            last = turn(ps[:, 4 + i, NJ * t:NJ * t + NJ], yt[0:NJ, t, P * i:P * i + P], NJ)
                        last.then_inc(sem("z_turned"), 1)
                    if h == 0:
                        conv(l, 1)
                pe.wait_ge(sem(f"z_ready{l}"), MC)
                step_in(at["glu", l])
                w = weights(at["glu", l])
                for m in range(MC):
                    for k in range(MC):
                        last = mm(ps[:, m, lat], w[:, k, P * m:P * m + P], aT[:, k, lat], k == 0, k == MC - 1)
                    last.then_inc(sem(f"glu_done{l}"), 1)
                pe.wait_ge(sem(f"conv_copied{l}"), MC)
                for m in range(MC):
                    last = mm(ps[:, 5, lat], ones[:], aT[:, MC + m, lat], m == 0, m == MC - 1)
                last.then_inc(sem(f"ln_sum{l}"), 1)
                for m in range(MC):
                    pe.wait_ge(sem(f"ln_sq{l}"), m + 1)
                    mm(ps[:, 6, lat], ones[:], sq[:, m % 2, lat], m == 0, m == MC - 1).then_inc(sem(f"ln_used{l}"), 1)
                pe.wait_ge(sem(f"go_ready{l}"), MC)
                project(n0 + 1, at["out", l], 512, lambda k: GO[:, k, lat] if k < MC else aT[:, k, lat],
                        lambda k: pe.wait_ge(sem(f"cv_ready{l}"), k - MC + 1) if k >= MC else None, KC, lat)
                norm(n0 + 1)
                norm(n0 + 2)
                if l == 0:
                    for i in range(FN):
                        n = at["ffn"] + i // 2
                        if i % 2 == 0:
                            step_in(n)
                        if i >= 3:
                            pe.wait_ge(sem("hid_ready"), i - 2)
                        for j in range(2):
                            w = weights(n, j)
                            for k in range(KC):
                                if i == 0 and j == 0:
                                    pe.wait_ge(sem("a_ready2"), 2 * k + 2)
                                last = mm(ps[:, 2 * (i % 3) + j, :], w[:, k, P * (i % 2):P * (i % 2) + P], aT[:, k, :],
                                          k == 0, k == KC - 1)
                        last.then_inc(sem("ffn_done"), 1)
                        if i == 6:
                            turn_c(1)
                    pe.wait_ge(sem("hid_ready"), FN)
                    project(3, at["down"], P, lambda k: hid[:, k, :], lambda k: None, FN, ALL)
                    norm(3)

            for tt in range(2):
                tok = slice(S + P * tt, S + P * tt + P)
                for k in range(KC):
                    if tt == 0:
                        pe.wait_ge(sem("a_ready6"), k + 1)
                    mm(ps[:, 4, NE * tt:NE * tt + NE], aT[:, k, tok], wr[:, k, :], k == 0, False)
                if tt == 0:
                    pe.wait_ge(sem("router_in"), 32)
                last = mm(ps[:, 4, NE * tt:NE * tt + NE], ones[0:1, :], br[:], False, True)
            last.then_inc(sem("logits"), 1)
            pe.wait_ge(sem("masked"), 2)
            mm(ps[:, 5, 0:NE], before[:], mask[:, 0], True, True)
            mm(ps[:, 5, NE:2 * NE], before[:], mask[:, 1], True, False)
            mm(ps[:, 5, NE:2 * NE], ones[:], mask[:, 0], False, True)
            mm(ps[:, 5, 2 * NE:3 * NE], ones[:], mask[:, 0], True, False)
            mm(ps[:, 5, 2 * NE:3 * NE], ones[:], mask[:, 1], False, True).then_inc(sem("counted"), 1)

            def experts(ph):
                g0 = ph * NE * NSTEP
                if ph:
                    pe.wait_ge(sem("acc_added"), 4 * NE + 1)
                for i in range(4):
                    for k in range(4):
                        last = turn(ps[:, i, P * k:P * k + P], aT[:, 4 * (i % 2) + k, S + P * (i // 2):S + P * (i // 2) + P])
                    last.then_inc(sem("ftok_turned"), 1)
                pe.wait_ge(sem("ftok_copied"), 4 * (ph + 1))
                pe.wait_ge(sem("selected"), 32 * (ph + 1))
                for i in range(16):
                    if i >= 4:
                        pe.wait_ge(sem("moved"), 20 * ph + i - 3)
                    for tt in range(2):
                        last = mm(ps[:, i % 4, :], ftok[:, tt, P * (i // 2):P * (i // 2) + P],
                                  Sel[:, tt, 4 * (i % 2):4 * (i % 2) + 4, :], tt == 0, tt == 1)
                    last.then_inc(sem("gathered"), 1)
                for i in range(4):
                    for j in range(4):
                        last = turn(ps[:, 4 + i, P * j:P * j + P], Sg[:, i // 2, 4 * (i % 2) + j, :])
                    last.then_inc(sem("gates_turned"), 1)
                pe.wait_ge(sem("moved"), 20 * (ph + 1))

                def down(e, o, c_):
                    g = g0 + o * NSTEP + c_
                    uses = DUSES[c_ % 3]
                    pe.wait_ge(sem(f"dn_in{c_ % 3}"), e * (16 * uses) + 16 * ((ph * NE + o) * uses + c_ // 3 + 1))
                    pe.wait_ge(sem("hide_ready"), e * NSTEP + (g + 1))
                    for f in range(2):
                        for nh in range(2):
                            last = mm(ps[:, 2 + nh, :], hide[:, c_ % 2, f, :], DN[c_ % 3][:, f, 512 * nh:512 * nh + 512],
                                      c_ == 0 and f == 0, c_ == NSTEP - 1 and f == 1)
                    last.then_inc(sem("dn_done"), 1)

                def spread(e, o):
                    pe.wait_ge(sem("ysb_ready"), e * 2 + 2 * (NE * ph + o + 1))
                    pe.wait_ge(sem("acc_added"), e * 4 + (4 * (NE * ph + o) + 1))
                    for k in range(KC):
                        rhs = Gt[:, bass.ds(e + o, 1), :].rearrange("p e t -> p (e t)")
                        last = mm(ps[:, 4 + k // 2, S * (k % 2):S * (k % 2) + S], ysb[:, P * k:P * k + P], rhs)
                        if k % 2:
                            last.then_inc(sem("spread"), 1)

                def expert(e, o):
                    for c_ in range(NSTEP):
                        g = g0 + o * NSTEP + c_
                        uses = USES[c_ % 4]
                        pe.wait_ge(sem(f"gu_in{c_ % 4}"), e * (32 * uses) + 32 * ((ph * NE + o) * uses + c_ // 4 + 1))
                        if c_ >= 2:
                            pe.wait_ge(sem("hide_ready"), e * NSTEP + (g - 1))
                        for j in range(2):
                            for f in range(2):
                                o_ = ps[:, c_ % 2, 256 * j + P * f:256 * j + P * f + P]
                                for k in range(KC):
                                    rhs = xg[:, bass.ds(e + o, 1), k, :].rearrange("p e s -> p (e s)")
                                    last = mm(o_, GU[c_ % 4][:, j, k, P * f:P * f + P], rhs, k == 0, k == KC - 1)
                        last.then_inc(sem("gu_done"), 1)
                        if c_ == 0 and o:
                            spread(e, o - 1)
                        if c_:
                            down(e, o, c_ - 1)
                    down(e, o, NSTEP - 1)

                expert(0, 0)
                with pe.Fori(0, NE - 1) as e:
                    expert(e, 1)
                spread(0, NE - 1)

            experts(0)
            pe.wait_ge(sem("routed"), 1)
            over = pe.value_load(most_i[0:1, 0:1], min_val=0, max_val=S)
            with pe.If(over > P):
                experts(1)
            norm(7)
            for i in range(4):
                for j in range(4):
                    k = 4 * (i % 2) + j
                    pe.wait_ge(sem("h_ready7"), k + 1)
                    last = turn(ps[:, i, P * j:P * j + P], hT[:, k, S + P * (i // 2):S + P * (i // 2) + P])
                last.then_inc(sem("out_turned"), 1)

        @block.vector
        def _(dve):
            count = [0]

            def link(ins):
                count[0] += 1
                ins.then_inc(sem("dve_chain"), 1)
                dve.wait_ge(sem("dve_chain"), count[0])

            def mark(ins):
                count[0] += 1
                ins.then_inc(sem("dve_chain"), 1)
                return count[0]

            def need(n):
                dve.wait_ge(sem("dve_chain"), n)

            tt_, ts_, stt = dve.tensor_tensor, dve.tensor_scalar, dve.scalar_tensor_tensor

            dve.wait_ge(sem("consts"), 7)
            link(dve.tensor_reduce(eyeh[:], ident[:].rearrange("p (s h) -> p h s", h=GH), AX_X, ALU.add))
            dve.wait_ge(sem("rows_in"), 16 * 16)
            dve.wait_ge(sem("dt"), 1)
            for i in range(2):
                for a in range(2):
                    ts_(rows_z[:, i, HP * a:HP * a + HP], rows_z[:, 2 + i, HP * a:HP * a + HP], dt[:, a:a + 1], None,
                        ALU.mult).then_inc(sem("z_rows"), 1)
            dve.tensor_copy(rows_d, load_d.rearrange("p l (s h) -> p l s h", s=1).broadcast_to([G, L, CL, GH]))\
                .then_inc(sem("z_rows"), 1)
            dve.wait_ge(sem("rows_turned"), 1)
            dve.tensor_copy(vT[:], ps[:, 0, 0:112]).then_inc(sem("par"), 1)
            dve.tensor_copy(bT[:], ps[:, 0, 128:128 + L * NM]).then_inc(sem("par"), 1)
            dve.tensor_copy(cwT[:], ps[:, 1, 0:MC * L * CW].rearrange("p (m k) -> p m k", m=MC)).then_inc(sem("par"), 1)
            dve.tensor_copy(dT[:], ps[:, 1, 256:256 + L * G].rearrange("p (l g) -> p l g", l=L)).then_inc(sem("par"), 1)
            dve.tensor_copy(zl, ps[:, 2, 0:256].rearrange("p (k x) -> p k x", k=4)).then_inc(sem("par"), 1)
            dve.wait_ge(sem("par"), 5)
            th = zl[:, 1]
            link(ts_(dz[:, 5], th, 1.0 / TWO_PI, ROUND, ALU.mult, ALU.add))
            link(ts_(dz[:, 5], dz[:, 5], -ROUND, None, ALU.add))
            link(stt(dz[:, 6], dz[:, 5], -TWO_PI_HI, th, ALU.mult, ALU.add))
            link(stt(dz[:, 7], dz[:, 5], -TWO_PI_MID, dz[:, 6], ALU.mult, ALU.add))
            link(stt(dz[:, 6], dz[:, 5], -TWO_PI_LO, dz[:, 7], ALU.mult, ALU.add))
            link(ts_(dz[:, 0], dz[:, 6], -PI, PI, ALU.max, ALU.min))
            link(stt(dz[:, 7], dz[:, 0], -1.0, dz[:, 0], ALU.mult, ALU.max))
            ts_(dz[:, 1], dz[:, 7], -1.0, TWO_PI / 4, ALU.mult, ALU.add).then_inc(sem("angle"), 1)
            lr, li = zl[:, 2], zl[:, 3]
            link(tt_(dz[:, 8], lr, lr, ALU.mult))
            link(tt_(dz[:, 9], li, li, ALU.mult))
            link(tt_(dz[:, 8], dz[:, 8], dz[:, 9], ALU.add))
            link(dve.reciprocal(dz[:, 9], dz[:, 8]))
            dve.wait_ge(sem("polar"), 3)
            p1r, p1i = dz[:, 10], dz[:, 11]
            link(tt_(p1r, dz[:, 2], dz[:, 4], ALU.mult))
            link(tt_(p1i, dz[:, 2], dz[:, 3], ALU.mult))
            link(ts_(dz[:, 12], p1r, -1.0, None, ALU.add))
            link(tt_(dz[:, 5], dz[:, 12], lr, ALU.mult))
            link(tt_(dz[:, 6], p1i, li, ALU.mult))
            link(tt_(dz[:, 5], dz[:, 5], dz[:, 6], ALU.add))
            link(tt_(cf[:, 0], dz[:, 5], dz[:, 9], ALU.mult))
            link(tt_(dz[:, 5], p1i, lr, ALU.mult))
            link(tt_(dz[:, 6], dz[:, 12], li, ALU.mult))
            link(tt_(dz[:, 5], dz[:, 5], dz[:, 6], ALU.subtract))
            link(tt_(cf[:, 1], dz[:, 5], dz[:, 9], ALU.mult))

            def powers(table, br_, bi_, n, past):
                view_ = lambda v: v.rearrange("p (l d q) -> p l d q", l=L, d=2)
                link(dve.memset(pc[:, 0], 1.0))
                link(dve.memset(pc[:, 1], 0.0))
                for p in range(n + 1):
                    cur, nxt = 2 * (p % 2), 2 * ((p + 1) % 2)
                    if p < n:
                        for r in range(2):
                            for d in range(2):
                                link(dve.tensor_copy(table[:, r, :, d, :, p if d == 0 else n - 1 - p],
                                                     view_(pc[:, cur + r])[:, :, d]))
                    elif past is not None:
                        link(dve.tensor_copy(past[:], pc[:, cur:cur + 2]))
                    if p < n and (p < n - 1 or past is not None):
                        link(tt_(pc[:, nxt], pc[:, cur], br_, ALU.mult))
                        link(tt_(dz[:, 5], pc[:, cur + 1], bi_, ALU.mult))
                        link(tt_(pc[:, nxt], pc[:, nxt], dz[:, 5], ALU.subtract))
                        link(tt_(pc[:, nxt + 1], pc[:, cur], bi_, ALU.mult))
                        link(tt_(dz[:, 5], pc[:, cur + 1], br_, ALU.mult))
                        link(tt_(pc[:, nxt + 1], pc[:, nxt + 1], dz[:, 5], ALU.add))

            powers(pw, p1r, p1i, CL + 1, None)
            link(dve.tensor_copy(a1[:], pc[:, 0:2]))
            powers(aw, a1[:, 0], a1[:, 1], NB, a8)
            for s_, t_ in ((a1, a1s), (a8, a8s)):
                link(ts_(t_[:, 0], s_[:, 1], -1.0, None, ALU.mult))
                link(dve.tensor_copy(t_[:, 1], s_[:, 1]))

            def load_tables(l):
                dve.wait_ge(sem("bc_in"), 16 * 40 * (l + 1))
                b = [Braw[:, r].rearrange("p d (q h) -> p (d q) h", h=GH) for r in range(2)]
                o = [Bb[:, r].rearrange("p d q h -> p (d q) h") for r in range(2)]
                t = std[:].rearrange("p (x h) -> p x h", h=GH)
                k = [cf[:, r, 32 * l:32 * l + 32].rearrange("p (x h) -> p x h", h=1).broadcast_to([P, 32, GH]) for r in range(2)]
                link(tt_(o[0], b[0], k[0], ALU.mult))
                link(tt_(t, b[1], k[1], ALU.mult))
                link(tt_(o[0], o[0], t, ALU.subtract))
                link(tt_(o[1], b[1], k[0], ALU.mult))
                link(tt_(t, b[0], k[1], ALU.mult))
                tt_(o[1], o[1], t, ALU.add).then_inc(sem("bb_ready"), 1)
                dve.wait_ge(sem("bb_ready"), l + 1)
                for r in range(2):
                    dve.wait_ge(sem("c_turned"), 2 * l + r + 1)
                    dve.tensor_copy(Ct[:, r].rearrange("p d q h -> p (d q h)"), ps[:, 5 + l + r, :]).then_inc(sem("c_copied"), 1)
                dve.wait_ge(sem("c_copied"), 2 * l + 2)

            def cmul(o, u, v, t):
                t = [b.rearrange("p (q s h) -> p q s h", s=o[0].shape[2], h=GH) for b in t]
                mark(tt_(o[0], u[0], v[0], ALU.mult))
                re = mark(tt_(t[0], u[1], v[1], ALU.mult))
                mark(tt_(o[1], u[0], v[1], ALU.mult))
                im = mark(tt_(t[1], u[1], v[0], ALU.mult))
                need(re)
                mark(tt_(o[0], o[0], t[0], ALU.subtract))
                need(im)
                return mark(tt_(o[1], o[1], t[1], ALU.add))

            def modulate():
                dve.wait_ge(sem("mod_turned"), N_ADA)
                tt_(modT[:].rearrange("p l m s -> p (l m) s"), ps[:, 7, 0:2 * L * NM].rearrange("p (m s) -> p m s", s=2),
                    bT[:].rearrange("p (m s) -> p m s", s=1).broadcast_to([P, L * NM, 2]), ALU.add).then_inc(sem("mod"), 1)
                dve.wait_ge(sem("mod"), 1)
                for l in range(L):
                    for i, (g0, m0, one) in enumerate(((0, 1, 1.0), (16, 2, 0.0), (32, 4, 1.0), (48, 5, 0.0))):
                        gain = vT[:, g0 + KC * l:g0 + KC * l + KC].rearrange("p (k s) -> p k s", s=1).broadcast_to([P, KC, 2])
                        link(stt(amp[:, l, i], modT[:, l, KC * m0:KC * m0 + KC, :], one, gain, ALU.add, ALU.mult))

            def out_table(l, h):
                if 2 * l + h:
                    dve.wait_ge(sem("y_chunks"), 4 * (2 * l + h))
                n = 4 * (CL + 1) * GH
                t = [b.rearrange("p i t -> p (i t)")[:, 0:n] for b in (sg[:], sq[:])] if h else \
                    [work[:, 15872:15872 + n], work[:, 15872 + n:15872 + 2 * n]]
                done = 0
                for d in range(2):
                    for q0 in range(0, HQ, 4):
                        qs = slice(HQ * h + q0, HQ * h + q0 + 4)
                        o = [E[:, d, r, q0:q0 + 4].rearrange("p q (s h) -> p q s h", h=GH) for r in range(2)]
                        u = [Ct[:, r, d, qs].rearrange("p q (s h) -> p q s h", s=1).broadcast_to([P, 4, CL + 1, GH])
                             for r in range(2)]
                        v = [pw[:, r, l, d, qs].rearrange("p q (s h) -> p q s h", h=1).broadcast_to([P, 4, CL + 1, GH])
                             for r in range(2)]
                        if done:
                            need(done)
                        done = cmul(o, u, v, t)
                    need(done)
                    ts_(E[:, d, 1], E[:, d, 1], -1.0, None, ALU.mult).then_inc(sem("out_table"), 1)

            def in_table(l, h, qq):
                n = 4 * l + 2 * h + qq
                if h and qq == 0:
                    dve.wait_ge(sem("y_chunks"), 4 * (2 * l + h))
                if n:
                    dve.wait_ge(sem("w_turned"), 4 * n)
                    dve.wait_ge(sem("r_done"), 4 * n)
                    dve.wait_ge(sem("r_ready"), n)
                for d in range(2):
                    qs = slice(HQ * h + 4 * qq, HQ * h + 4 * qq + 4)
                    o = [Fq[:, d, r].rearrange("p q (s h) -> p q s h", h=GH) for r in range(2)]
                    u = [Bb[:, r, d, qs].rearrange("p q (s h) -> p q s h", s=1).broadcast_to([P, 4, CL, GH]) for r in range(2)]
                    back = slice(CL - 1, None, -1) if d == 0 else slice(CL, 0, -1)
                    v = [pw[:, r, l, d, qs, back].rearrange("p q (s h) -> p q s h", h=1).broadcast_to([P, 4, CL, GH])
                         for r in range(2)]
                    if d:
                        need(done)
                    done = cmul(o, u, v, (std[:], rstd[:] if n else sg[:, 0, :]))
                need(done)
                ts_(tick[:], eps_t[:], 0.0, None, ALU.mult).then_inc(sem("f_ready"), 1)

            def toeplitz(l, h, qq):
                n = 4 * l + 2 * h + qq
                if n:
                    dve.wait_ge(sem("k_in"), 16 * 15 * n)
                if qq == 0 and 2 * l + h:
                    dve.wait_ge(sem("z_turned"), 2 * (2 * l + h))
                for i in range(4):
                    dve.wait_ge(sem("r_done"), 4 * n + i + 1)
                    dve.tensor_copy(R[:, i // 2, i % 2], ps[:, 4 + i, :].rearrange("p (q x) -> p q x", q=4))\
                        .then_inc(sem("r_copied"), 1)
                dve.wait_ge(sem("r_copied"), 4 * n + 4)
                diag = R[:, 0, :, :, 0:GH]
                link(tt_(diag, diag, R[:, 1, :, :, P - GH:P], ALU.add))
                t = std[:, 0:P].rearrange("p (a q h) -> p a q h", a=2, h=GH)
                g0 = 2 * (HQ * h + 4 * qq)
                dd = dT[:, l, g0:g0 + 8].rearrange("p (q a h) -> p a q h", a=2, h=1).broadcast_to([P, 2, 4, GH])
                ey = eyeh[:].rearrange("p (a q h) -> p a q h", a=1, q=1).broadcast_to([P, 2, 4, GH])
                link(tt_(t, ey, dd, ALU.mult))
                tt_(diag, diag, t, ALU.add).then_inc(sem("r_ready"), 1)

            def norm(n):
                cs = norm_cols(n)
                dve.wait_ge(sem("std_ready"), n + 1)
                link(dve.reciprocal(rstd[:, cs], std[:, cs]))

            norm(0)
            load_tables(0)
            out_table(0, 0)
            in_table(0, 0, 0)
            modulate()

            def scale(n):
                if n:
                    norm(n)
                for k in range(KC):
                    for s, cs in streams(norm_cols(n)):
                        stt(aT[:, k, cs], hT[:, k, cs], amp[:, n // 4, n % 4, k, s:s + 1], rstd[:, cs], ALU.mult, ALU.mult)\
                            .then_inc(sem(f"scaled{n}"), 1)

            def add_back(n, y):
                norm(n)
                ss = streams(norm_cols(n))
                for k in range(KC):
                    for s, cs in ss:
                        stt(y(k, cs), y(k, cs), amp[:, n // 4, n % 4, k, s:s + 1], rstd[:, cs], ALU.mult, ALU.mult)\
                            .then_inc(sem(f"y_scaled{n}"), 1)
                    if k:
                        dve.wait_ge(sem(f"y_scaled{n}"), len(ss) * k)
                        cs = norm_cols(n)
                        tt_(hT[:, k - 1, cs], hT[:, k - 1, cs], y(k - 1, cs), ALU.add).then_inc(sem(f"h_ready{n}"), 1)
                dve.wait_ge(sem(f"y_scaled{n}"), len(ss) * KC)
                cs = norm_cols(n)
                tt_(hT[:, KC - 1, cs], hT[:, KC - 1, cs], y(KC - 1, cs), ALU.add).then_inc(sem(f"h_ready{n}"), 1)

            def copy_y(n, y):
                for m in range(KC):
                    dve.wait_ge(sem(f"y_done{n}"), m + 1)
                    dve.tensor_copy(y(m, norm_cols(n)), ps[:, m % 4, norm_cols(n)]).then_inc(sem(f"y_copied{n}"), 1)

            def recur(l, h):
                qs = slice(HQ * h, HQ * h + HQ)

                def coef(table, d):
                    v = table[:].rearrange("p r (l d q) -> p r l d q", l=L, d=2)
                    return v[:, :, l, d, qs]

                Xv = [X[:, d].rearrange("p r q (b i) -> p r q b i", i=NB) for d in range(2)]
                shape = [P, 2, HQ, NB]
                re = [coef(a1, d)[:, 0:1].rearrange("p r (q j) -> p r q j", j=1).broadcast_to(shape) for d in range(2)]
                im = [coef(a1s, d).rearrange("p r (q j) -> p r q j", j=1).broadcast_to(shape) for d in range(2)]
                t = [[tS[:, d, i].rearrange("p r (q j) -> p r q j", j=NB) for i in range(2)] for d in range(2)]
                added = [0, 0]
                for s in range(1, NB):
                    o = [Xv[0][:, :, :, :, s], Xv[1][:, :, :, :, NB - 1 - s]]
                    prev = [Xv[0][:, :, :, :, s - 1], Xv[1][:, :, :, :, NB - s]]
                    made = [0, 0]
                    for d in range(2):
                        if s > 1:
                            need(added[d])
                        mark(tt_(t[d][0], prev[d], re[d], ALU.mult))
                        made[d] = mark(tt_(t[d][1], prev[d][:, ::-1], im[d], ALU.mult))
                    for i in range(2):
                        for d in range(2):
                            need(made[d] if i == 0 else added[d])
                            added[d] = mark(tt_(o[d], o[d], t[d][i], ALU.add))
                need(added[1])
                flat = lambda v: v.rearrange("p r q b -> p (r q) b")
                perm = gcar.rearrange("p b d r q -> p d (r q) b")
                mark(dve.tensor_copy(perm[:, 0], flat(Xv[0][:, :, :, :, NB - 1])))
                mark(dve.tensor_copy(perm[:, 1, :, 0:4], flat(Xv[1][:, :, :, 3::-1, 0])))
                link(dve.tensor_copy(perm[:, 1, :, 4:8], flat(Xv[1][:, :, :, 7:3:-1, 0])))
                ga = a8[:].rearrange("p r (l d q) -> p l d r q", l=L, d=2)[:, l, :, :, qs]
                gs = a8s[:].rearrange("p r (l d q) -> p l d r q", l=L, d=2)[:, l, :, :, qs]
                gt = [tS[:, 0, i, :, 0:2 * HQ].rearrange("p r (d q) -> p d r q", d=2) for i in range(2)]
                for s in range(1, NB):
                    o, prev = gcar[:, s], gcar[:, s - 1]
                    mark(tt_(gt[0], prev, ga[:, :, 0:1].broadcast_to([P, 2, 2, HQ]), ALU.mult))
                    link(tt_(gt[1], prev[:, :, ::-1], gs, ALU.mult))
                    link(tt_(o, o, gt[0], ALU.add))
                    link(tt_(o, o, gt[1], ALU.add))
                gq = gpre.rearrange("p d r q b -> p d (r q) b")
                mark(dve.memset(gq[:, 0, :, 0:1], 0.0))
                mark(dve.memset(gq[:, 1, :, 3:4], 0.0))
                mark(dve.tensor_copy(gq[:, 0, :, 1:8], perm[:, 0, :, 0:7]))
                mark(dve.tensor_copy(gq[:, 1, :, 2::-1], perm[:, 1, :, 0:3]))
                link(dve.tensor_copy(gq[:, 1, :, 7:3:-1], perm[:, 1, :, 3:7]))
                shape = [P, HQ, NB, NB]
                dve.wait_ge(sem("k_in"), 16 * 15 * 2 * (2 * l + h + 1))
                for d in range(2):
                    prods = [work[:, 12800 + 512 * j:13312 + 512 * j].rearrange("p (q b i) -> p q b i", q=HQ, b=NB)
                             for j in range(4)]
                    for r in range(2):
                        for i in range(2):
                            g = gpre[:, d, r if i == 0 else 1 - r].rearrange("p q (b i) -> p q b i", i=1).broadcast_to(shape)
                            k = aw[:, i, l, d, qs].rearrange("p q (b i) -> p q b i", b=1).broadcast_to(shape)
                            made = mark(tt_(prods[2 * r + i], g, k, ALU.mult))
                    for r in range(2):
                        need(made - 2 + 2 * r)
                        o = Pst[:, d, r].rearrange("p q (b i) -> p q b i", b=NB)
                        summed = mark(tt_(o, prods[2 * r], prods[2 * r + 1], ALU.subtract if r == 0 else ALU.add))
                    for r in range(2):
                        need(summed - 1 + r)
                        ov = Pst[:, d, r].rearrange("p q (b i) -> p (q b) i", b=NB)
                        xv = X[:, d, r].rearrange("p q (b i) -> p (q b) i", b=NB)
                        to, fr = (slice(1, NB), slice(0, NB - 1)) if d == 0 else (slice(0, NB - 1), slice(1, NB))
                        last = mark(tt_(ov[:, :, to], ov[:, :, to], xv[:, :, fr], ALU.add))
                    if d == 1:
                        need(last)
                ts_(tick[:], eps_t[:], 0.0, None, ALU.mult).then_inc(sem("p_ready"), 1)

            for l in range(L):
                lat = LAT if l else ALL
                n0 = 4 * l
                scale(n0)
                if l:
                    dve.wait_ge(sem("scaled4"), KC * len(streams(norm_cols(4))))
                    in_table(l, 0, 0)
                else:
                    dve.wait_ge(sem("scaled0"), KC * 2)
                toeplitz(l, 0, 0)
                for i in range(8):
                    dve.wait_ge(sem(f"u_turned{l}"), i + 1)
                    src = ps[0:HP, i % 4, :].rearrange("p (g j b) -> p b g j", g=4, b=2)
                    dve.tensor_copy(U[0:HP, 4 * i:4 * i + 4, :], src[:, 0])
                    dve.tensor_copy(U[HP:P, 4 * i:4 * i + 4, :], src[:, 1]).then_inc(sem(f"u_copied{l}"), 1)
                in_table(l, 0, 1)
                for m in range(MC):
                    dve.wait_ge(sem(f"vg_sig{l}"), m + 1)
                    st = slice(1, 2) if l else slice(0, 2)
                    tt_(apad[:, m, st, PAD:PAD + S], ps[:, 4 + 2 * (m % 2), lat].rearrange("p (i t) -> p i t", t=S),
                        sg[:, m % 2, lat].rearrange("p (i t) -> p i t", t=S), ALU.mult).then_inc(sem(f"gated{l}"), 1)
                toeplitz(l, 0, 1)
                for h in range(2):
                    if h:
                        in_table(l, 1, 0)
                        out_table(l, 1)
                        toeplitz(l, 1, 0)
                        in_table(l, 1, 1)
                        toeplitz(l, 1, 1)
                    dve.wait_ge(sem("x_states"), 4 * (2 * l + h + 1))
                    recur(l, h)
                for m in range(MC):
                    dve.wait_ge(sem(f"glu_sig{l}"), m + 1)
                    tt_(GO[:, m, lat], aT[:, m, lat], sg[:, m % 2, lat], ALU.mult).then_inc(sem(f"glu_used{l}"), 1)
                dve.wait_ge(sem(f"glu_used{l}"), MC)
                ts_(tick[:], eps_t[:], 0.0, None, ALU.mult).then_inc(sem(f"go_ready{l}"), MC)
                dve.wait_ge(sem(f"ln_sum{l}"), 1)
                link(ts_(rstd[:, lat], ps[:, 5, lat], 1.0 / DS, None, ALU.mult))
                for m in range(MC):
                    tt_(aT[:, MC + m, lat], aT[:, MC + m, lat], rstd[:, lat], ALU.subtract).then_inc(sem(f"centred{l}"), 1)
                dve.wait_ge(sem(f"ln_std{l}"), 1)
                dve.wait_ge(sem(f"centred{l}"), MC)
                link(dve.reciprocal(rstd[:, lat], std[:, lat]))
                for m in range(MC):
                    tt_(aT[:, MC + m, lat], aT[:, MC + m, lat], rstd[:, lat], ALU.mult).then_inc(sem(f"ln_scaled{l}"), 1)
                copy_y(n0 + 1, lambda k, cs: yE[:, k, cs])
                add_back(n0 + 1, lambda k, cs: yE[:, k, cs])
                dve.wait_ge(sem(f"h_ready{n0 + 1}"), KC)
                scale(n0 + 2)
                if l == 0:
                    for i in range(FN):
                        dve.wait_ge(sem("ffn_silu"), i + 1)
                        tt_(hid[:, i, :], sg[:, i % 2, :], ps[:, 2 * (i % 3) + 1, :], ALU.mult).then_inc(sem("hid_ready"), 1)
                        if i == 8:
                            load_tables(1)
                        if i == 10:
                            out_table(1, 0)
                    copy_y(3, lambda k, cs: aT[:, k, cs])
                    add_back(3, lambda k, cs: aT[:, k, cs])
                    dve.wait_ge(sem("h_ready3"), KC)

            dve.memset(acc, 0.0).then_inc(sem("acc_added"), 1)
            dve.wait_ge(sem("logits"), 1)
            link(dve.tensor_copy(lg[:], ps[:, 4, 0:2 * NE].rearrange("p (i e) -> p i e", i=2)))
            for i in range(2):
                link(dve.max(top[:, i], lg[:, i]))
                link(dve.max_index(topi[:, i], top[:, i], lg[:, i]))
            link(dve.tensor_copy(topf[:], topi[:]))
            for i in range(2):
                for j in range(2):
                    link(ts_(hot[:, i, j], iota_s[:, 0:NE], topf[:, i, j:j + 1], None, ALU.is_equal))
            tt_(gw[:, :, 0:1], top[:, :, 1:2], top[:, :, 0:1], ALU.subtract).then_inc(sem("top2"), 1)
            for i in range(2):
                tt_(mask[:, i], hot[:, i, 0], hot[:, i, 1], ALU.add).then_inc(sem("masked"), 1)
            dve.wait_ge(sem("gate_exp"), 1)
            link(ts_(gw[:, :, 2:3], gw[:, :, 1:2], 1.0, None, ALU.add))
            link(dve.reciprocal(gw[:, :, 3:4], gw[:, :, 2:3]))
            link(tt_(gw[:, :, 2:3], gw[:, :, 1:2], gw[:, :, 3:4], ALU.mult))
            for i in range(2):
                link(ts_(gate[:, i], hot[:, i, 0], gw[:, i, 3:4], None, ALU.mult))
                link(stt(gate[:, i], hot[:, i, 1], gw[:, i, 2:3], gate[:, i], ALU.mult, ALU.add))
            dve.wait_ge(sem("counted"), 1)
            dve.wait_ge(sem("masked"), 2)
            link(stt(slot_of[:], ps[:, 5, 0:2 * NE].rearrange("p (i e) -> p i e", i=2), UNROUTED, mask[:], ALU.add, ALU.mult))
            link(ts_(slot_of[:], slot_of[:], -UNROUTED, None, ALU.add))
            link(dve.tensor_reduce(most[:], ps[:, 5, 2 * NE:3 * NE], AX_X, ALU.max))
            dve.tensor_copy(most_i[:], most[:]).then_inc(sem("routed"), 1)

            def experts(ph):
                if ph:
                    ts_(slot_of[:], slot_of[:], -float(P), None, ALU.add).then_inc(sem("slots_down"), 1)
                    dve.wait_ge(sem("slots_down"), 1)
                for i in range(4):
                    dve.wait_ge(sem("ftok_turned"), 4 * ph + i + 1)
                    dve.tensor_copy(ftok[:, i // 2, 512 * (i % 2):512 * (i % 2) + 512], ps[:, i, :])\
                        .then_inc(sem("ftok_copied"), 1)
                for i in range(2):
                    for e in range(NE):
                        ts_(Sel[:, i, e, :], iota_s[:], slot_of[:, i, e:e + 1], None, ALU.is_equal).then_inc(sem("selected"), 1)
                        ts_(Sg[:, i, e, :], iota_s[:], slot_of[:, i, e:e + 1], gate[:, i, e:e + 1], ALU.is_equal, ALU.mult)\
                            .then_inc(sem("selected"), 1)
                def add(e, o):
                    for i in range(4):
                        dve.wait_ge(sem("spread"), e * 4 + (4 * (NE * ph + o) + i + 1))
                        a = acc[:, 2 * i:2 * i + 2, :].rearrange("p k t -> p (k t)")
                        tt_(a, a, ps[:, 4 + i, :], ALU.add).then_inc(sem("acc_added"), 1)

                def expert(e, o):
                    for c_ in range(NSTEP):
                        g = (ph * NE + o) * NSTEP + c_
                        dve.wait_ge(sem("sge_ready"), e * NSTEP + (g + 1))
                        if c_ >= 2:
                            dve.wait_ge(sem("dn_done"), e * NSTEP + (g - 1))
                        tt_(hide[:, c_ % 2], sge[:, c_ % 2, :].rearrange("p (f s) -> p f s", f=2),
                            ps[:, c_ % 2, 256:512].rearrange("p (f s) -> p f s", f=2), ALU.mult).then_inc(sem("hide_ready"), 1)
                        if c_ == 0 and o:
                            add(e, o - 1)
                    dve.wait_ge(sem("dn_done"), e * NSTEP + (ph * NE + o + 1) * NSTEP)
                    dve.tensor_copy(ysb[:, 512:1024], ps[:, 3, :]).then_inc(sem("ysb_ready"), 1)

                expert(0, 0)
                with dve.Fori(0, NE - 1) as e:
                    expert(e, 1)
                add(0, NE - 1)
                dve.wait_ge(sem("acc_added"), 4 * NE * (ph + 1) + 1)

            dve.wait_ge(sem("acc_added"), 1)
            experts(0)
            dve.wait_ge(sem("routed"), 1)
            over = dve.value_load(most_i[0:1, 0:1], min_val=0, max_val=S)
            with dve.If(over > P):
                experts(1)
            ts_(tick[:], eps_t[:], 0.0, None, ALU.mult).then_inc(sem("summed"), 1)
            add_back(7, lambda k, cs: acc[:, k, :])
            for i in range(4):
                dve.wait_ge(sem("out_turned"), i + 1)
                ins = dve.tensor_copy(hT[:, 4 * (i // 2) + 2 * (i % 2):4 * (i // 2) + 2 * (i % 2) + 2, 0:S],
                                      ps[:, i, :].rearrange("p (k t) -> p k t", t=S))
                link(ins) if i % 2 == 0 else ins.then_inc(sem("rows_out"), 1)


_INS = ["x", "c", "ctx", "c_ctx", "w_ada", "b_ada", "g_pre_mix", "g_post_mix", "g_pre_ffn", "g_post_ffn", "w_in",
        "ssm_lam_re", "ssm_lam_im", "ssm_log_dt", "ssm_b_re", "ssm_b_im", "ssm_c_re", "ssm_c_im", "ssm_d",
        "ssm_w_glu", "ssm_b_glu", "conv_w", "conv_b", "conv_ln_g", "conv_ln_b", "w_out", "ffn_w_gate", "ffn_w_up",
        "ffn_w_down", "moe_w_router", "moe_b_router", "moe_w_gate", "moe_w_up", "moe_w_down"]
_OUTS = [((1, 256, 1024), "float32")]


def kernel(**inputs):
    import numpy as _np
    import concourse.bacc as _bacc
    from concourse import mybir as _mybir
    from concourse.bass_utils import run_bass_kernel_spmd as _run

    nc = _bacc.Bacc("TRN2", target_bir_lowering=False, num_devices=1)
    arrays, args = {}, []
    for name in _INS:
        a = _np.ascontiguousarray(inputs[name])
        arrays[f"in_{name}_dram"] = a
        args.append(nc.dram_tensor(f"in_{name}_dram", a.shape, _mybir.dt.from_np(a.dtype), kind="ExternalInput").ap())
    for i, (shape, dtype) in enumerate(_OUTS):
        dt = _mybir.dt.from_np(_np.dtype(dtype))
        args.append(nc.dram_tensor(f"out_{i}_dram", shape, dt, kind="ExternalOutput").ap())
    hybrid_backbone(nc, *args)
    r = _run(nc, [arrays], core_ids=[0])
    got = tuple(r.results[0][f"out_{i}_dram"] for i in range(len(_OUTS)))
    return got[0]
```
